# Optimizing a Trainium2 kernel written in Bass

```python
import jax, jax.numpy as jnp
from jax import lax
import numpy as np

D_MODEL = 1024
BATCH = 1
SEQ = 256
DEPTH = 2
DEC_BATCH = 8
DEC_SEQ = 4
PAST_LEN = 256
PAGE_SIZE = 128

N_HEADS = 8
HEAD_DIM = D_MODEL // N_HEADS
IDX_HEADS = 8
IDX_DIM = 64
IDX_TOPK = 256
IDX_QBLOCK = 64
ATTN_SCALE = HEAD_DIM ** -0.5
ATTN_SPLITS = (N_HEADS * HEAD_DIM,
               2 * N_HEADS * HEAD_DIM,
               3 * N_HEADS * HEAD_DIM,
               3 * N_HEADS * HEAD_DIM + IDX_HEADS * IDX_DIM,
               3 * N_HEADS * HEAD_DIM + IDX_HEADS * IDX_DIM + IDX_DIM)
ATTN_IN = 3 * N_HEADS * HEAD_DIM + IDX_HEADS * IDX_DIM + IDX_DIM + IDX_HEADS
GM_CHUNK = 128
GM_WIDTH = D_MODEL
GM_GROUPS = 8
GM_GROUP_DIM = GM_WIDTH // GM_GROUPS
D_FF = 2816
N_EXPERTS = 8
TOP_K_EXPERTS = 2
D_FF_EXPERT = 3584
N_ATTN_LAYERS = (DEPTH + 1) // 2
N_GMLP_LAYERS = DEPTH // 2
EPS = 1e-6
NEG = -1e30

kernel_name = 'dsa_gmlp_hybrid_step'

def rms_norm(x, g):
    xf = x.astype(jnp.float32)
    y = xf * lax.rsqrt(jnp.mean(xf * xf, axis=-1, keepdims=True) + EPS)
    return (y * g.astype(jnp.float32)).astype(x.dtype)

def layer_norm(x, g, b):
    xf = x.astype(jnp.float32)
    mu = jnp.mean(xf, axis=-1, keepdims=True)
    var = jnp.mean(jnp.square(xf - mu), axis=-1, keepdims=True)
    y = (xf - mu) * lax.rsqrt(var + EPS)
    return (y * g.astype(jnp.float32) + b.astype(jnp.float32)).astype(x.dtype)

def swiglu(h, w_gate, w_up, w_down):
    return (jax.nn.silu(h @ w_gate) * (h @ w_up)) @ w_down

def attn_project(h, w_in, g_q, g_k, g_kidx):
    B, T, _ = h.shape
    q, k, v, qi, ki, wi = jnp.split(h @ w_in, ATTN_SPLITS, axis=-1)
    q = rms_norm(q.reshape(B, T, N_HEADS, HEAD_DIM), g_q)
    k = rms_norm(k.reshape(B, T, N_HEADS, HEAD_DIM), g_k)
    v = v.reshape(B, T, N_HEADS, HEAD_DIM)
    qi = qi.reshape(B, T, IDX_HEADS, IDX_DIM)
    ki = rms_norm(ki, g_kidx)
    return q, k, v, qi, ki, wi

def index_scores(qi, ki, wi):
    logits = jnp.einsum('bthd,bsd->bths', qi, ki).astype(jnp.float32) * IDX_DIM ** -0.5
    w = wi.astype(jnp.float32) * IDX_HEADS ** -0.5
    return jnp.einsum('bth,bths->bts', w, jax.nn.relu(logits))

def dsa_prompt(q, k, v, qi, ki, wi, topk):
    B, S = q.shape[0], q.shape[1]
    n_blocks = S // IDX_QBLOCK
    spos = jnp.arange(S)
    take_rows = jax.vmap(lambda rows, idx: rows[idx])

    def block(bi):
        t0 = bi * IDX_QBLOCK
        qb = lax.dynamic_slice_in_dim(q, t0, IDX_QBLOCK, axis=1)
        qib = lax.dynamic_slice_in_dim(qi, t0, IDX_QBLOCK, axis=1)
        wib = lax.dynamic_slice_in_dim(wi, t0, IDX_QBLOCK, axis=1)
        tpos = t0 + jnp.arange(IDX_QBLOCK)
        score = index_scores(qib, ki, wib)
        score = jnp.where(spos[None, None, :] <= tpos[None, :, None], score, NEG)
        _, idx = lax.top_k(score, topk)
        k_sel = take_rows(k, idx)
        v_sel = take_rows(v, idx)
        s = jnp.einsum('bthd,btkhd->bthk', qb, k_sel).astype(jnp.float32) * ATTN_SCALE
        valid = (idx <= tpos[None, :, None])[:, :, None, :]
        p = jax.nn.softmax(jnp.where(valid, s, NEG), axis=-1)
        return jnp.einsum('bthk,btkhd->bthd', p, v_sel).astype(q.dtype)

    o = lax.map(block, jnp.arange(n_blocks))
    return jnp.moveaxis(o, 0, 1).reshape(B, S, N_HEADS, HEAD_DIM)

def dsa_sample(q, k, v, qi, ki, wi, cache_k, cache_v, cache_kidx, page_table, topk):
    Bd, T = q.shape[0], q.shape[1]
    n_pages = page_table.shape[1]
    past = n_pages * PAGE_SIZE
    ki_past = cache_kidx[page_table].reshape(Bd, past, IDX_DIM)
    ki_all = jnp.concatenate([ki_past, ki.astype(ki_past.dtype)], axis=1)
    tpos = past + jnp.arange(T)
    spos = jnp.arange(past + T)
    score = index_scores(qi, ki_all, wi)
    score = jnp.where(spos[None, None, :] <= tpos[None, :, None], score, NEG)
    _, idx = lax.top_k(score, topk)
    valid = (idx <= tpos[None, :, None])[:, :, None, :]
    is_new = (idx >= past)[:, :, None, :]
    page_idx = jnp.minimum(idx // PAGE_SIZE, n_pages - 1)
    phys = jax.vmap(lambda pt, pi: pt[pi])(page_table, page_idx)
    off = idx % PAGE_SIZE
    k_sel = cache_k[phys, off]
    v_sel = cache_v[phys, off]
    onehot = (idx[..., None] == tpos[None, None, None, :]).astype(jnp.float32)
    s_pool = jnp.einsum('bthd,btkhd->bthk', q, k_sel).astype(jnp.float32)
    s_new_all = jnp.einsum('bthd,bjhd->bthj', q, k).astype(jnp.float32)
    s_new = jnp.einsum('bthj,btkj->bthk', s_new_all, onehot)
    s = jnp.where(is_new, s_new, s_pool) * ATTN_SCALE
    p = jax.nn.softmax(jnp.where(valid, s, NEG), axis=-1)
    p_pool = jnp.where(is_new, 0.0, p)
    p_new = jnp.einsum('bthk,btkj->bthj', p, onehot)
    o = jnp.einsum('bthk,btkhd->bthd', p_pool, v_sel) + jnp.einsum('bthj,bjhd->bthd', p_new, v)
    return o.astype(q.dtype)

def gmlp_mixer(h, w_in, ln_g, ln_b, w_s, b_s, w_out):
    B, T, _ = h.shape
    u, v = jnp.split(jax.nn.gelu(h @ w_in, approximate=False), 2, axis=-1)
    v = layer_norm(v, ln_g, ln_b)
    tc = min(T, GM_CHUNK)
    vg = v.reshape(B, T // tc, tc, GM_GROUPS, GM_GROUP_DIM)
    ws = w_s[:, :tc, :tc] * jnp.tril(jnp.ones((tc, tc), w_s.dtype))
    mixed = jnp.einsum('gij,bcjgd->bcigd', ws, vg) + b_s[:, :tc].T[None, None, :, :, None]
    return (u * mixed.reshape(B, T, GM_WIDTH)) @ w_out, v

def moe_swiglu(h, w_router, w_gate, w_up, w_down):
    shape = h.shape
    t = h.reshape(-1, shape[-1])
    logits = (t @ w_router).astype(jnp.float32)
    top_logits, top_idx = lax.top_k(logits, TOP_K_EXPERTS)
    gates = jax.nn.softmax(top_logits, axis=-1)
    combine = jnp.sum(jax.nn.one_hot(top_idx, N_EXPERTS, dtype=jnp.float32) * gates[..., None], axis=1)
    out = jnp.zeros_like(t)
    for e in range(N_EXPERTS):
        out = out + combine[:, e:e + 1].astype(t.dtype) * swiglu(t, w_gate[e], w_up[e], w_down[e])
    return out.reshape(shape)

def setup_inputs(seed: int = 0) -> dict:
    key = jax.random.key(seed)
    ks = jax.random.split(key, 26)
    n_pages = PAST_LEN // PAGE_SIZE
    n_pool = (DEC_BATCH * n_pages * 5) // 4
    NA, NB = N_ATTN_LAYERS, N_GMLP_LAYERS

    def nrm(k, shape, scale=1.0):
        return jax.random.normal(k, shape, jnp.float32) * scale

    page_table = jax.random.permutation(ks[5], n_pool)[: DEC_BATCH * n_pages]
    page_table = page_table.reshape(DEC_BATCH, n_pages).astype(jnp.int32)
    return {
        'x_prompt': nrm(ks[0], (BATCH, SEQ, D_MODEL)),
        'x_sample': nrm(ks[1], (DEC_BATCH, DEC_SEQ, D_MODEL)),
        'cache_k': nrm(ks[2], (NA, n_pool, PAGE_SIZE, N_HEADS, HEAD_DIM)),
        'cache_v': nrm(ks[3], (NA, n_pool, PAGE_SIZE, N_HEADS, HEAD_DIM)),
        'cache_kidx': nrm(ks[4], (NA, n_pool, PAGE_SIZE, IDX_DIM)),
        'page_table': page_table,
        'norm_mix': 1.0 + nrm(ks[6], (DEPTH, D_MODEL), 0.02),
        'norm_ffn': 1.0 + nrm(ks[7], (DEPTH, D_MODEL), 0.02),
        'attn_w_in': nrm(ks[8], (NA, D_MODEL, ATTN_IN), D_MODEL ** -0.5),
        'attn_g_q': 1.0 + nrm(ks[9], (NA, HEAD_DIM), 0.02),
        'attn_g_k': 1.0 + nrm(ks[10], (NA, HEAD_DIM), 0.02),
        'attn_g_kidx': 1.0 + nrm(ks[11], (NA, IDX_DIM), 0.02),
        'attn_w_out': nrm(ks[12], (NA, N_HEADS * HEAD_DIM, D_MODEL), (N_HEADS * HEAD_DIM) ** -0.5),
        'gm_w_in': nrm(ks[13], (NB, D_MODEL, 2 * GM_WIDTH), D_MODEL ** -0.5),
        'gm_ln_g': 1.0 + nrm(ks[14], (NB, GM_WIDTH), 0.02),
        'gm_ln_b': nrm(ks[15], (NB, GM_WIDTH), 0.02),
        'gm_w_s': nrm(ks[16], (NB, GM_GROUPS, GM_CHUNK, GM_CHUNK), GM_CHUNK ** -0.5),
        'gm_b_s': 1.0 + nrm(ks[17], (NB, GM_GROUPS, GM_CHUNK), 0.1),
        'gm_w_out': nrm(ks[18], (NB, GM_WIDTH, D_MODEL), GM_WIDTH ** -0.5),
        'ffn_w_gate': nrm(ks[19], (NA, D_MODEL, D_FF), D_MODEL ** -0.5),
        'ffn_w_up': nrm(ks[20], (NA, D_MODEL, D_FF), D_MODEL ** -0.5),
        'ffn_w_down': nrm(ks[21], (NA, D_FF, D_MODEL), D_FF ** -0.5),
        'moe_w_router': nrm(ks[22], (NB, D_MODEL, N_EXPERTS), D_MODEL ** -0.5),
        'moe_w_gate': nrm(ks[23], (NB, N_EXPERTS, D_MODEL, D_FF_EXPERT), D_MODEL ** -0.5),
        'moe_w_up': nrm(ks[24], (NB, N_EXPERTS, D_MODEL, D_FF_EXPERT), D_MODEL ** -0.5),
        'moe_w_down': nrm(ks[25], (NB, N_EXPERTS, D_FF_EXPERT, D_MODEL), D_FF_EXPERT ** -0.5),
    }

def reference(x_prompt, x_sample, cache_k, cache_v, cache_kidx, page_table,
              norm_mix, norm_ffn, attn_w_in, attn_g_q, attn_g_k, attn_g_kidx, attn_w_out,
              gm_w_in, gm_ln_g, gm_ln_b, gm_w_s, gm_b_s, gm_w_out,
              ffn_w_gate, ffn_w_up, ffn_w_down,
              moe_w_router, moe_w_gate, moe_w_up, moe_w_down):
    xp, xs = x_prompt, x_sample
    B, S, _ = xp.shape
    T = xs.shape[1]
    past = page_table.shape[1] * PAGE_SIZE
    topk_prompt = min(IDX_TOPK, S // 4)
    topk_sample = min(IDX_TOPK, (past + T) // 4)
    k_prompt, v_prompt, kidx_prompt = [], [], []
    k_sample, v_sample, kidx_sample, gm_v_sample = [], [], [], []
    for i in range(DEPTH):
        j = i // 2
        hp = rms_norm(xp, norm_mix[i])
        hs = rms_norm(xs, norm_mix[i])
        if i % 2 == 0:
            qp, kp, vp, qip, kip, wip = attn_project(hp, attn_w_in[j], attn_g_q[j], attn_g_k[j], attn_g_kidx[j])
            op = dsa_prompt(qp, kp, vp, qip, kip, wip, topk_prompt)
            qs, ks_, vs_, qis, kis, wis = attn_project(hs, attn_w_in[j], attn_g_q[j], attn_g_k[j], attn_g_kidx[j])
            os_ = dsa_sample(qs, ks_, vs_, qis, kis, wis, cache_k[j], cache_v[j], cache_kidx[j],
                             page_table, topk_sample)
            xp = xp + op.reshape(B, S, -1) @ attn_w_out[j]
            xs = xs + os_.reshape(xs.shape[0], T, -1) @ attn_w_out[j]
            n_pp = B * S // PAGE_SIZE
            k_prompt.append(kp.reshape(n_pp, PAGE_SIZE, N_HEADS, HEAD_DIM))
            v_prompt.append(vp.reshape(n_pp, PAGE_SIZE, N_HEADS, HEAD_DIM))
            kidx_prompt.append(kip.reshape(n_pp, PAGE_SIZE, IDX_DIM))
            k_sample.append(ks_)
            v_sample.append(vs_)
            kidx_sample.append(kis)
            xp = xp + swiglu(rms_norm(xp, norm_ffn[i]), ffn_w_gate[j], ffn_w_up[j], ffn_w_down[j])
            xs = xs + swiglu(rms_norm(xs, norm_ffn[i]), ffn_w_gate[j], ffn_w_up[j], ffn_w_down[j])
        else:
            op, _ = gmlp_mixer(hp, gm_w_in[j], gm_ln_g[j], gm_ln_b[j], gm_w_s[j], gm_b_s[j], gm_w_out[j])
            os_, v_gm = gmlp_mixer(hs, gm_w_in[j], gm_ln_g[j], gm_ln_b[j], gm_w_s[j], gm_b_s[j], gm_w_out[j])
            xp = xp + op
            xs = xs + os_
            gm_v_sample.append(v_gm)
            xp = xp + moe_swiglu(rms_norm(xp, norm_ffn[i]), moe_w_router[j], moe_w_gate[j], moe_w_up[j], moe_w_down[j])
            xs = xs + moe_swiglu(rms_norm(xs, norm_ffn[i]), moe_w_router[j], moe_w_gate[j], moe_w_up[j], moe_w_down[j])
    return (xp, xs, jnp.stack(k_prompt), jnp.stack(v_prompt), jnp.stack(kidx_prompt),
            jnp.stack(k_sample), jnp.stack(v_sample), jnp.stack(kidx_sample), jnp.stack(gm_v_sample))


_drawn_inputs = setup_inputs


def setup_inputs(seed=0):
    import zlib

    import numpy as np

    out = dict(_drawn_inputs(seed))
    spreads = {}
    factors = {'gm_ln_b': 8.215, 'gm_ln_g': 2.868, 'attn_g_q': 3.345}
    for name, (base, spread) in spreads.items():
        noise = np.random.default_rng([zlib.crc32(name.encode()), seed]).standard_normal(out[name].shape)
        drawn = base * np.exp(spread * noise) if base else spread * noise
        out[name] = __import__('jax').numpy.asarray(drawn.astype(out[name].dtype))
    for name, factor in factors.items():
        out[name] = (out[name] * factor).astype(out[name].dtype)
    return out
```

```python
from contextlib import ExitStack

import concourse.bass as bass
from concourse import mybir
from concourse.alu_op_type import AluOpType as ALU

F32 = mybir.dt.float32
I32 = mybir.dt.int32
ACT = mybir.ActivationFunctionType
AX = mybir.AxisListType

P = 128
D = 1024
KD = D // P
NP = 256
NSEQ, TS = 8, 4
NS = NSEQ * TS
T = NP + NS
ROWS = [P, P, NS]
H, HD = 8, 128
IH, ID = 8, 64
PAST = 256
PAGES = PAST // P
WS = PAST + TS
TOPK_P, TOPK_S = 64, 65
DFF, DFE = 2816, 3584
NFB = DFF // P
E = 8
CH = 512
NCH = DFE // CH
SLOT = KD * CH
RING = 7
EPS = 1e-6
NEG = -1e30
MARK = -3e38
MARKED = -2e38
SCALE = HD ** -0.5
MAXBLK = (T + P - 1) // P
ITEMS = E * MAXBLK
FAR = 1000.0


class Bank:

    def __init__(self, banks, full, freed):
        self.banks, self.full_sem, self.freed_sem = banks, full, freed
        self.order, self.index = [], {}

    def add(self, name, consumer):
        self.index[name] = len(self.order)
        self.order.append(consumer)

    def ap(self, name):
        return self.banks[self.index[name] % len(self.banks)]

    def full(self, name):
        return self.full_sem, self.index[name] + 1

    def freed(self, name):
        n = self.index[name]
        who = self.order[n]
        return self.freed_sem[who], self.order[:n + 1].count(who)

    def free_sem(self, name):
        return self.freed_sem[self.order[self.index[name]]]

    def room(self, engine, name):
        n = self.index[name] - len(self.banks)
        if n >= 0:
            who = self.order[n]
            engine.wait_ge(self.freed_sem[who], self.order[:n + 1].count(who))


def build(nc, a, out):
    ctx = ExitStack()

    def sem(name):
        return ctx.enter_context(nc.semaphore(name))

    def sb(name, shape, dt=F32, stack=None):
        return (stack or ctx).enter_context(nc.sbuf_tensor(name, shape, dt))

    ring = sb("ring", [P, RING, SLOT])
    xT = sb("xT", [P, KD, T])
    hT = sb("hT", [P, KD, T])
    ident = sb("ident", [P, P])
    ones = sb("ones", [P, P])
    upper = sb("upper", [P, P])
    iota = sb("iota", [P, P])
    bmask = sb("bmask", [NS, NSEQ])
    vmask3 = sb("vmask3", [NS, TS, NSEQ])
    vmask = sb("vmask", [NS, TS])
    selm = sb("selm", [P, 2, NS])
    rep32 = sb("rep32", [NS, P])
    rep8 = sb("rep8", [IH, P])
    rep4 = sb("rep4", [TS, NS])
    epst = sb("epst", [P, 1])
    small = sb("small", [35, P])
    gT = sb("gT", [P, 35])
    rt = sb("rt", [P, T])

    early = ExitStack()
    tok = sb("tok", [P, 3, D], stack=early)
    wi = sb("wi", [P, 2, IH], stack=early)
    wiT = sb("wiT", [IH, NS], stack=early)
    selw = sb("selw", [P, 2, NS], stack=early)
    kiT = sb("kiT", [P, T], stack=early)
    kitok = sb("kitok", [P, 3, ID], stack=early)
    sc0 = sb("sc0", [P, P], stack=early)
    sc1 = sb("sc1", [P, NP], stack=early)
    scs = sb("scs", [NS, WS], stack=early)
    m8 = sb("m8", [P, 8], stack=early)
    madd_s = sb("madd_s", [NS, PAST + NS], stack=early)
    madd_t = sb("madd_t", [NS, TS], stack=early)
    maddr = sb("maddr", [P, PAST + NS], stack=early)
    big = sb("big", [P, 6 * CH], stack=early)
    rl = big[:].rearrange("p (g c) -> p g c", g=6)
    ktok = big[:].rearrange("p (m c) -> p m c", m=3)
    stS = big[:, 0:CH]
    stN = big[0:NS, CH:CH + H * NS]
    sPT = big[:, 2 * CH:2 * CH + 6 * P].rearrange("p (g c) -> p g c", g=2)
    idx = ExitStack()
    qiz = sb("qiz", [P, IH, T], stack=idx)
    qix = sb("qix", [P, NSEQ, IH, TS], stack=idx)
    kip = sb("kip", [P, NSEQ * PAGES, 2, ID], stack=idx)
    kipT = sb("kipT", [P, NSEQ * PAGES, P], stack=idx)
    kip0 = sb("kip0", [P, NSEQ * PAGES, ID], stack=idx)
    kisq = sb("kisq", [P, T], stack=idx)
    rls = sb("rls", [P, 2, WS], stack=idx)
    selm4 = sb("selm4", [P, 2, NS, IH], stack=idx)
    idx.close()
    qT = sb("qT", [P, H, T], stack=early)
    kT = sb("kT", [P, H, T], stack=early)
    sq2 = sb("sq2", [P, 2, T], stack=early)
    rt2 = sb("rt2", [P, 2, T], stack=early)
    KT = sb("KT", [P, 2, H, P], stack=early)
    sm = sb("sm", [P, 2, CH], stack=early)
    st = sb("st", [P, 4, 8], stack=early)
    PT = sb("PT", [P, 2, CH], stack=early)
    pt_i = sb("pt_i", [1, NSEQ * PAGES], I32, stack=early)
    early.close()

    ffn = ExitStack()
    hh = sb("hh", [P, NFB, T], stack=ffn)
    sg = sb("sg", [P, 2, T], stack=ffn)
    ffn.close()

    gm = ExitStack()
    gv = sb("gv", [P, 3, D], stack=gm)
    gu = sb("gu", [P, KD, T], stack=gm)
    lng = sb("lng", [P, D], stack=gm)
    lnb = sb("lnb", [P, D], stack=gm)
    wsr = sb("wsr", [P, 8, P], stack=gm)
    wsT = sb("wsT", [P, 8, P], stack=gm)
    wsS = sb("wsS", [NS, 8, NS], stack=gm)
    wst4 = sb("wst4", [NS, 8, TS], stack=gm)
    bsb = sb("bsb", [P, 8, P], stack=gm)
    bn = sb("bn", [P, 3, 12], stack=gm)
    mv = sb("mv", [P, 3, 4], stack=gm)
    gm.close()

    moe = ExitStack()
    xtok = sb("xtok", [P, 3, D], stack=moe)
    htok = sb("htok", [P, 3, D], stack=moe)
    wr = sb("wr", [P, KD, E], stack=moe)
    lg = sb("lg", [P, 3, 2 * E], stack=moe)
    wk = sb("wk", [P, 3, 2 * E], stack=moe)
    r8 = sb("r8", [P, 3, 8], stack=moe)
    l8 = sb("l8", [P, 3, 8], stack=moe)
    sel = sb("sel", [P, 3, E], stack=moe)
    ex = sb("ex", [P, 3, E], stack=moe)
    cden = sb("cden", [P, 3, 4], stack=moe)
    pos = sb("pos", [P, 3, E], stack=moe)
    slot_of = sb("slot_of", [P, 3, ITEMS + E], stack=moe)
    comb = sb("comb", [P, 3, ITEMS + E], stack=moe)
    cnt = sb("cnt", [P, 8], stack=moe)
    cnt_i = sb("cnt_i", [1, 1], I32, stack=moe)
    pick = sb("pick", [P, 3, P], stack=moe)
    pickg = sb("pickg", [P, 3, P], stack=moe)
    pgT = sb("pgT", [P, T], stack=moe)
    xg = sb("xg", [P, KD, P], stack=moe)
    sge = sb("sge", [P, 2, CH], stack=moe)
    he = sb("he", [P, 2, CH], stack=moe)
    heT = sb("heT", [P, 2, CH], stack=moe)
    ysb = sb("ysb", [P, D], stack=moe)
    moe.close()

    banks = [ctx.enter_context(nc.psum_tensor(f"bank{i}", [P, 512], F32)) for i in range(8)]

    a_full, a_act, a_dve = sem("a_full"), sem("a_act"), sem("a_dve")
    b_full, b_act, b_dve = sem("b_full"), sem("b_act"), sem("b_dve")
    A = Bank(banks[0:6], a_full, {"act": a_act, "dve": a_dve})
    B = Bank(banks[6:8], b_full, {"act": b_act, "dve": b_dve})
    w_in = [sem(f"w_in{i}") for i in range(RING)]
    x_in = [sem(f"x_in{i}") for i in range(3)]
    par_in, pt_in, kip_in, gm_in, wr_in, ws_in = (sem(n) for n in
        ("par_in", "pt_in", "kip_in", "gm_in", "wr_in", "ws_in"))
    const, zeros, chain, achain, pchain = (sem(n) for n in ("const", "zeros", "chain", "achain", "pchain"))
    sq_act, sq_dve, root, h_ready = (sem(n) for n in ("sq_act", "sq_dve", "root", "h_ready"))
    par_ok, kisq_ok, kiroot, kiT_ok, kip2_ok = (sem(n) for n in ("par_ok", "kisq_ok", "kiroot", "kiT_ok", "kip2_ok"))
    score_ok, masked, smask_ok, selw_ok = (sem(n) for n in ("score_ok", "masked", "smask_ok", "selw_ok"))
    qsq, qroot, qk_ok = (sem(n) for n in ("qsq", "qroot", "qk_ok"))
    neg_ok, exp_ok, p_ok = (sem(n) for n in ("neg_ok", "exp_ok", "p_ok"))
    kt_free, part_used = sem("kt_free"), sem("part_used")
    stored = sem("stored")
    ln_ok, lnroot, ws_ok, wsS_ok = (sem(n) for n in ("ln_ok", "lnroot", "ws_ok", "wsS_ok"))
    mk_ok, mix_ok, ln_bad = (sem(n) for n in ("mk_ok", "mix_ok", "ln_bad"))
    moe_zero, neg_m1, ex_ok, sel_ok, items_ok = (sem(n) for n in ("moe_zero", "neg_m1", "ex_ok", "sel_ok", "items_ok"))
    g_full, u_full, d_used, t_full, pg_full, ga_full, sc_full = (sem(n) for n in
        ("g_full", "u_full", "d_used", "t_full", "pg_full", "ga_full", "sc_full"))
    sg_ok, he_ok, heT_ok, xg_ok, pgT_ok, y_ok, pick_ok, pickg_ok, sc_ok = (sem(n) for n in
        ("sg_ok", "he_ok", "heT_ok", "xg_ok", "pgT_ok", "y_ok", "pick_ok", "pickg_ok", "sc_ok"))

    NU = 6
    unit_tile = [0, 0, 1, 1, 1, 1]
    unit_heads = [range(0, 4), range(4, 8), range(0, 2), range(2, 4), range(4, 6), range(6, 8)]
    A.add("par", "dve")
    for c in range(KD):
        A.add(("xt", c), "act" if c % 2 == 0 else "dve")
    B.add(("ssq", 0), "act")
    for p in range(4):
        A.add(("qi", p), "act" if p % 2 == 0 else "dve")
    A.add("ki", "dve")
    A.add("wi", "dve")
    B.add("kissq", "act")
    A.add("wrep", "dve")
    for q in range(4):
        A.add(("kipt", q), "act")
    A.add("kio", "act")
    for g in range(2):
        A.add(("iss", g), "act")
    A.add("isel", "dve")
    for g in range(6):
        A.add(("is", g), "act")
    for n in range(16):
        A.add(("qk", n), "dve")
        if n:
            B.add(("qkn", n - 1), "act")
    B.add(("qkn", 15), "act")
    for half in range(2):
        for m in range(3):
            A.add(("v", m, half), "act")
    for m in range(3):
        for half in range(2):
            A.add(("kt", m, half), "act")
    B.add("st", "act")
    B.add("stn", "act")
    for b in range(NSEQ):
        if b < NU:
            A.add(("s", b), "dve")
        for pg in range(PAGES):
            A.add(("ktr", b, pg, 0), "act")
            A.add(("ktr", b, pg, 1), "dve")
        if 1 <= b <= NU:
            A.add(("pt", b - 1), "act")
        if 2 <= b <= NU + 1:
            A.add(("o", b - 2), "act")
    A.add("mrep", "dve")
    for g in range(2):
        A.add(("ss", g), "dve")
    for g in range(2):
        A.add(("spt", g), "act")
    B.add("so", "act")
    for m in range(KD):
        A.add(("wo", m), "dve")
    B.add(("ssq", 1), "act")
    for f in range(NFB):
        A.add(("fg", f), "act")
        A.add(("fu", f), "dve")
    for m in range(KD):
        A.add(("fd", m), "dve")
    B.add(("ssq", 2), "act")
    for q in range(2):
        A.add(("wst", q), "act")
    A.add("wsr", "dve")
    for half in range(2):
        for m in range(3):
            A.add(("gv", m, half), "act")
    for c in range(KD):
        A.add(("gu", c), "act")
    for g in range(8):
        A.add(("mix", g), "dve")
    for m in range(KD):
        A.add(("go", m), "dve")
    B.add(("ssq", 3), "act")
    for m in range(3):
        for half in range(2):
            A.add(("xo", m, half), "act")
    A.add("rt", "dve")
    for m in range(3):
        for half in range(2):
            A.add(("ho", m, half), "act")
    A.add("pos", "dve")

    def cols(w, c0, n):
        return w[:, c0:c0 + n].rearrange("(k p) f -> p k f", p=P)

    def tile_cols(slot, n):
        return ring[:, slot, 0:KD * n].rearrange("p (k f) -> p k f", k=KD)

    w_att, w_o = a["attn_w_in"][0], a["attn_w_out"][0]
    w_fg, w_fu, w_fd = a["ffn_w_gate"][0], a["ffn_w_up"][0], a["ffn_w_down"][0]
    w_gi, w_go = a["gm_w_in"][0], a["gm_w_out"][0]
    Q0, K0, V0, QI0 = 0, H * HD, 2 * H * HD, 3 * H * HD
    KI0 = QI0 + IH * ID
    WI0 = KI0 + ID
    SMALLW = 2 * ID + IH
    stream = [("qi", A.full(("qi", 3))), ("kiwi", A.full("wi"))]
    stream += [(("q", i), A.full(("qk", 4 * i + 3))) for i in range(2)]
    stream += [(("k", i), A.full(("qk", 8 + 4 * i + 3))) for i in range(2)]
    stream += [(("v", i), A.full(("v", 2, i))) for i in range(2)]
    stream += [(("kp", i), A.full(("ktr", 2 * i + 1, 1, 1))) for i in range(4)]
    stream += [(("vp", i), (part_used, i + 1) if i < 3 else B.full("so")) for i in range(4)]
    stream += [(("wo", i), A.full(("wo", 4 * i + 3))) for i in range(2)]
    for i in range(6):
        last = min(4 * i + 3, NFB - 1)
        stream += [(("fg", i), A.full(("fg", last))), (("fu", i), A.full(("fu", last)))]
    for half in range(2):
        for part in range(3):
            over = (part_used, 3 + 2 * half + part + 1) if part < 2 else A.full(("fd", 4 * half + 3))
            stream += [(("fd", half, part), over)]
    stream += [(("gv", i), A.full(("gv", 2, i))) for i in range(2)]
    stream += [(("gu", i), A.full(("gu", 4 * i + 3))) for i in range(2)]
    stream += [(("go", i), A.full(("go", 4 * i + 3))) for i in range(2)]
    N0 = len(stream)
    slot, arrived_at, per_slot = {}, {}, [0] * RING
    for n, (name, _) in enumerate(stream):
        slot[name] = n % RING
        per_slot[n % RING] += 3 if name == "kiwi" else PAGES * 2 if name[0] in ("kp", "vp") else 1
        arrived_at[name] = (w_in[n % RING], 16 * per_slot[n % RING])
    base_count = list(per_slot)

    def w3(name, n=CH, k=KD):
        return ring[:, slot[name], 0:k * n].rearrange("p (k f) -> p k f", k=k)

    def expert_slot(t):
        return (N0 + t) % RING

    def expert_arrival(i, t):
        s = expert_slot(t)
        return w_in[s], 16 * (base_count[s] + t // RING + 1) + i * (16 * 3)

    BASE = {g_full: NCH, u_full: NCH, d_used: NCH, t_full: NCH, pg_full: 1, sg_ok: NCH, he_ok: NCH,
            heT_ok: NCH, pgT_ok: 1, y_ok: 2, sc_ok: 6}

    def start_counters(engine, *sems):
        for s in sems:
            engine.sem_inc(s, BASE[s])

    PER_ITEM = 3 * NCH
    assert PER_ITEM == 3 * RING

    x_prompt, x_sample = a["x_prompt"][0], a["x_sample"].rearrange("b t d -> (b t) d")
    n_pool = a["cache_k"].shape[1]
    cache = {"kp": a["cache_k"][0].rearrange("n s h d -> n s (h d)"),
             "vp": a["cache_v"][0].rearrange("n s h d -> n s (h d)")}
    o_y = out["y_prompt"][0], out["y_sample"].rearrange("b t d -> (b t) d")
    o_k = (out["k_prompt"][0].rearrange("n s h d -> (n s) (h d)"),
           out["k_sample"][0].rearrange("b t h d -> (b t) (h d)"))
    o_v = (out["v_prompt"][0].rearrange("n s h d -> (n s) (h d)"),
           out["v_sample"][0].rearrange("b t h d -> (b t) (h d)"))
    o_ki = (out["kidx_prompt"][0].rearrange("n s d -> (n s) d"),
            out["kidx_sample"][0].rearrange("b t d -> (b t) d"))
    o_gv = out["gm_v_sample"][0].rearrange("b t d -> (b t) d")
    N_STORED = 0

    def rows_of(pair, m):
        return pair[0][P * m:P * m + P, :] if m < 2 else pair[1]

    block = ctx.enter_context(nc.Block())

    @block.sync
    def _(sp):
        sp.dma_start(pt_i[0:1, :], a["page_table"].rearrange("(o b) n -> o (b n)", o=1)).then_inc(pt_in, 16)
        pages = None
        for n, (name, _) in enumerate(stream):
            if n >= RING:
                sp.wait_ge(*stream[n - RING][1])
            s, got = n % RING, w_in[n % RING]
            if name == "qi":
                sp.dma_start(tile_cols(s, CH), cols(w_att, QI0, CH)).then_inc(got, 16)
            elif name == "kiwi":
                t = tile_cols(s, SMALLW)
                sp.dma_start(t[:, :, 0:ID], cols(w_att, KI0, ID)).then_inc(got, 16)
                sp.dma_start(t[:, :, ID:2 * ID], cols(w_att, KI0, ID)).then_inc(got, 16)
                sp.dma_start(t[:, :, 2 * ID:SMALLW], cols(w_att, WI0, IH)).then_inc(got, 16)
            elif name[0] in ("q", "k", "v"):
                c0 = {"q": Q0, "k": K0, "v": V0}[name[0]] + CH * name[1]
                sp.dma_start(tile_cols(s, CH), cols(w_att, c0, CH)).then_inc(got, 16)
            elif name[0] in ("kp", "vp"):
                if pages is None:
                    sp.wait_ge(pt_in, 16)
                    pages = True
                for j in range(2 * PAGES):
                    pg = sp.value_load(pt_i[0:1, 4 * name[1] + j:4 * name[1] + j + 1], min_val=0, max_val=n_pool - 1)
                    src = cache[name[0]][bass.ds(pg, 1), :, :].rearrange("o s c -> (o s) c")
                    sp.dma_start(ring[:, s, D * j:D * j + D], src).then_inc(got, 16)
            elif name[0] == "wo":
                sp.dma_start(tile_cols(s, CH), cols(w_o, CH * name[1], CH)).then_inc(got, 16)
            elif name[0] in ("fg", "fu"):
                w = w_fg if name[0] == "fg" else w_fu
                width = min(CH, DFF - CH * name[1])
                sp.dma_start(tile_cols(s, width), cols(w, CH * name[1], width)).then_inc(got, 16)
            elif name[0] == "fd":
                _, half, part = name
                k = min(8, NFB - 8 * part)
                src = w_fd[1024 * part:1024 * part + P * k, CH * half:CH * half + CH]
                sp.dma_start(ring[:, s, 0:k * CH].rearrange("p (k f) -> p k f", k=k),
                             src.rearrange("(k p) f -> p k f", p=P)).then_inc(got, 16)
            elif name[0] in ("gv", "gu"):
                c0 = (D if name[0] == "gv" else 0) + CH * name[1]
                sp.dma_start(tile_cols(s, CH), cols(w_gi, c0, CH)).then_inc(got, 16)
            elif name[0] == "go":
                sp.dma_start(tile_cols(s, CH), cols(w_go, CH * name[1], CH)).then_inc(got, 16)

        def expert_tile(e, t):
            s, c, kind = expert_slot(t), t // 3, t % 3
            if kind < 2:
                w = a["moe_w_gate" if kind == 0 else "moe_w_up"][0]
                src = w[bass.ds(e, 1), :, CH * c:CH * c + CH].rearrange("o (k p) f -> p (o k) f", p=P)
                sp.dma_start(tile_cols(s, CH), src).then_inc(w_in[s], 16)
            else:
                src = a["moe_w_down"][0][bass.ds(e, 1), CH * c:CH * c + CH, :]
                sp.dma_start(ring[:, s, :].rearrange("p (k f) -> p k f", k=CH // P),
                             src.rearrange("o (k p) f -> p (o k) f", p=P)).then_inc(w_in[s], 16)

        for t in range(PER_ITEM):
            n = N0 + t - RING
            if n < N0:
                sp.wait_ge(*stream[n][1])
            else:
                c, kind = (t - RING) // 3, (t - RING) % 3
                sp.wait_ge((g_full, u_full, d_used)[kind], c + 1 + NCH)
            expert_tile(0, t)
        sp.wait_ge(items_ok, 1)
        n_items = sp.value_load(cnt_i[0:1, 0:1], min_val=E, max_val=ITEMS)
        with sp.Fori(1, n_items) as i:
            at = i * NCH + NCH
            for t in range(PER_ITEM):
                c, kind = (t - RING) // 3, (t - RING) % 3
                sp.wait_ge((g_full, u_full, d_used)[kind], at + (c + 1))
                expert_tile(i % E, t)

    @block.gpsimd
    def _(pool):
        done = [0]

        def link(ins):
            done[0] += 1
            ins.then_inc(pchain, 1)
            pool.wait_ge(pchain, done[0])

        def memsets(*pairs):
            for t, v in pairs:
                last = nc.gpsimd.memset(t, v)
            link(last)

        def select(t, op, fill, base, pattern, cm):
            return nc.gpsimd.affine_select(out=t, in_=t, compare_op=op, fill=fill, base=base, pattern=pattern,
                                           channel_multiplier=cm)

        memsets((ident[:], 0.0), (ones[:], 1.0), (epst[:], EPS))
        select(ident[:], ALU.not_equal, 1.0, 0, [[-1, P]], 1).then_inc(const, 1)
        for t in (qiz, qix):
            last = nc.gpsimd.memset(t[:], 0.0)
        last.then_inc(zeros, 1)
        memsets((rep8[:], 0.0), (selm4[:], 0.0), (rep32[:], 0.0), (rep4[:], 0.0), (bmask[:], 1.0),
                (vmask3[:], 1.0), (upper[:], 1.0))
        select(rep8[:].rearrange("k (j h t) -> k j h t", j=4, h=IH), ALU.not_equal, 1.0, 0,
               [[0, 4], [-1, IH], [0, TS]], 1)
        for g in range(2):
            select(selm4[:, g, :, :].rearrange("p (b t) h -> p b t h", t=TS), ALU.not_equal, 1.0, P * g,
                   [[-NS, NSEQ], [-1, TS], [-TS, IH]], 1)
        select(rep32[:].rearrange("k (j q) -> k j q", j=4), ALU.not_equal, 1.0, 0, [[0, 4], [-1, NS]], 1)
        select(rep4[:].rearrange("k (b t) -> k b t", t=TS), ALU.not_equal, 1.0, 0, [[0, NSEQ], [-1, TS]], 1)
        select(upper[:], ALU.is_ge, 0.0, -1, [[1, P]], -1)
        select(bmask[:], ALU.is_ge, 0.0, 0, [[-TS, NSEQ]], 1)
        link(select(vmask3[:], ALU.is_ge, 0.0, 0, [[-1, TS], [-TS, NSEQ]], 1))
        select(bmask[:], ALU.is_ge, 0.0, TS - 1, [[TS, NSEQ]], -1)
        select(vmask3[:], ALU.is_ge, 0.0, TS - 1, [[0, TS], [TS, NSEQ]], -1)
        nc.gpsimd.iota(iota[:], [[1, P]], base=0, channel_multiplier=0,
                       allow_small_or_imprecise_dtypes=True).then_inc(const, 1)
        pool.wait_ge(kip_in, 16 * NSEQ * PAGES)
        for j in range(2):
            last = nc.gpsimd.tensor_copy(kip[:, :, j, :], kip0[:, :, :])
        last.then_inc(kip2_ok, 1)
        pool.wait_ge(score_ok, 2)
        select(sc0[:], ALU.is_ge, NEG, 0, [[-1, P]], 1)
        select(sc1[:], ALU.is_ge, NEG, P, [[-1, NP]], 1).then_inc(masked, 1)
        pool.wait_ge(smask_ok, 2)
        select(sc0[:], ALU.is_ge, NEG, 0, [[-1, P]], 1)
        select(sc1[:], ALU.is_ge, NEG, P, [[-1, NP]], 1).then_inc(masked, 1)
        pool.wait_ge(*A.freed(("wst", 1)))
        select(wsT[:], ALU.is_ge, 0.0, 0, [[0, 8], [1, P]], -1).then_inc(ws_ok, 1)
        pool.wait_ge(*A.freed(("go", KD - 1)))
        for t, v in ((slot_of, -FAR), (comb, 0.0), (lg, MARK), (l8, MARK), (pgT, 0.0), (ysb, 0.0)):
            last = nc.gpsimd.memset(t[:], v)
        last.then_inc(moe_zero, 1)

    @block.scalar
    def _(act):
        nonlocal N_STORED
        done = [0]

        def link(ins):
            done[0] += 1
            ins.then_inc(achain, 1)
            act.wait_ge(achain, done[0])

        def copy(dst, src):
            return nc.scalar.activation(dst, src, ACT.Copy)

        def store(dst, src):
            nonlocal N_STORED
            N_STORED += 1
            act.dma_start(dst, src).then_inc(stored, 16)

        start_counters(act, sg_ok, heT_ok, pgT_ok, y_ok)
        for m in range(3):
            src = x_prompt[P * m:P * m + P, :] if m < 2 else x_sample
            act.dma_start(tok[0:ROWS[m], m, :], src).then_inc(x_in[m], 16)
        for r, w in enumerate((a["norm_mix"][0], a["norm_ffn"][0], a["norm_mix"][1], a["norm_ffn"][1])):
            act.dma_start(small[8 * r:8 * r + 8, :], w.rearrange("(c p) -> c p", p=P)).then_inc(par_in, 16)
        act.dma_start(small[32:33, :], a["attn_g_q"]).then_inc(par_in, 16)
        act.dma_start(small[33:34, :], a["attn_g_k"]).then_inc(par_in, 16)
        act.dma_start(small[34:35, 0:ID], a["attn_g_kidx"]).then_inc(par_in, 16)
        act.dma_start(small[34:35, ID:P], a["attn_g_kidx"]).then_inc(par_in, 16)
        act.wait_ge(pt_in, 16)
        for j in range(NSEQ * PAGES):
            pg = act.value_load(pt_i[0:1, j:j + 1], min_val=0, max_val=n_pool - 1)
            act.dma_start(kip0[:, j, :], a["cache_kidx"][0][bass.ds(pg, 1), :, :].rearrange("o s d -> (o s) d"))\
               .then_inc(kip_in, 16)

        def squares_and_root(n, xt_ready):
            act.wait_ge(*xt_ready)
            nc.scalar.activation(hT[:, 0:4, :], xT[:, 0:4, :], ACT.Square).then_inc(sq_act, 1)
            act.wait_ge(*B.full(("ssq", n)))
            nc.scalar.activation(rt[:], B.ap(("ssq", n))[:, 0:T], ACT.Sqrt, bias=epst[:, 0:1], scale=1.0 / D)\
              .then_inc(b_act, 1)

        for c in range(0, KD, 2):
            act.wait_ge(*A.full(("xt", c)))
            copy(xT[:, c, :], A.ap(("xt", c))[:, 0:T]).then_inc(a_act, 1)
        act.wait_ge(const, 1)
        act.wait_ge(*A.freed(("xt", KD - 2)))
        squares_and_root(0, A.freed(("xt", KD - 1)))
        act.wait_ge(zeros, 1)
        for p in (0, 2):
            act.wait_ge(*A.full(("qi", p)))
            bank = A.ap(("qi", p))
            for j in range(2):
                h, r = 2 * p + j, slice(ID * j, ID * j + ID)
                copy(qiz[r, h, :], bank[r, 0:T])
                last = copy(qix[r, :, h, :], bank[r, NP:T].rearrange("p (b t) -> p b t", t=TS))
            last.then_inc(a_act, 1)
        act.wait_ge(*A.full("ki"))
        nc.scalar.activation(kisq[:], A.ap("ki")[:, 0:T], ACT.Square).then_inc(kisq_ok, 1)
        act.wait_ge(*B.full("kissq"))
        act.wait_ge(h_ready, KD)
        nc.scalar.activation(rt[:], B.ap("kissq")[:, 0:T], ACT.Sqrt, bias=epst[:, 0:1], scale=1.0 / P)\
          .then_inc(b_act, 1)
        for q in range(4):
            act.wait_ge(*A.full(("kipt", q)))
            copy(kipT[:, 4 * q:4 * q + 4, :], A.ap(("kipt", q))[:].rearrange("p (a s) -> p a s", a=4)).then_inc(a_act, 1)
        act.wait_ge(*A.full("kio"))
        kio = A.ap("kio")[:, 0:3 * P].rearrange("p (m d) -> p m d", m=3)
        copy(kitok[:, 0:2, :], kio[:, 0:2, 0:ID])
        copy(kitok[0:NS, 2, :], kio[0:NS, 2, 0:ID]).then_inc(a_act, 1)
        act.wait_ge(*A.freed("kio"))
        for m in range(3):
            store(rows_of(o_ki, m), kitok[0:ROWS[m], m, :])
        for g in range(2):
            act.wait_ge(*A.full(("iss", g)))
            nc.scalar.activation(rls[:, g, :], A.ap(("iss", g))[:, 0:WS], ACT.Relu, scale=ID ** -0.5).then_inc(a_act, 1)
        for g in range(6):
            act.wait_ge(*A.full(("is", g)))
            nc.scalar.activation(rl[:, g, :], A.ap(("is", g))[:], ACT.Relu, scale=ID ** -0.5).then_inc(a_act, 1)
        for n in range(17):
            if n < 16:
                act.wait_ge(*A.full(("qk", n)))
                if n >= 2:
                    act.wait_ge(*B.full(("qkn", n - 2)))
                nc.scalar.activation(sq2[:, n % 2, :], A.ap(("qk", n))[:, 0:T], ACT.Square).then_inc(qsq, 1)
            if n >= 1:
                j = n - 1
                act.wait_ge(*B.full(("qkn", j)))
                if j >= 2:
                    act.wait_ge(*A.freed(("qk", j - 2)))
                nc.scalar.activation(rt2[:, j % 2, :], B.ap(("qkn", j))[:, 0:T], ACT.Sqrt, bias=epst[:, 0:1],
                                     scale=1.0 / HD).then_inc(b_act, 1)
        for half in range(2):
            for m in range(3):
                act.wait_ge(*A.full(("v", m, half)))
                r = ROWS[m]
                copy(tok[0:r, m, CH * half:CH * half + CH], A.ap(("v", m, half))[0:r, :]).then_inc(a_act, 1)
        act.wait_ge(*A.freed(("v", 2, 1)))
        for m in range(3):
            store(rows_of(o_v, m), tok[0:ROWS[m], m, :])
        for m in range(3):
            for half in range(2):
                act.wait_ge(*A.full(("kt", m, half)))
                r = ROWS[m]
                copy(ktok[0:r, m, CH * half:CH * half + CH], A.ap(("kt", m, half))[0:r, :]).then_inc(a_act, 1)
        act.wait_ge(*A.freed(("kt", 2, 1)))
        for m in range(3):
            store(rows_of(o_k, m), ktok[0:ROWS[m], m, :])

        def exps(u, rows, nh, w):
            act.wait_ge(neg_ok, u + 1)
            for j in range(nh):
                last = nc.scalar.activation(sm[0:rows, u % 2, w * j:w * j + w], sm[0:rows, u % 2, w * j:w * j + w],
                                            ACT.Exp, bias=st[0:rows, 2 * (u % 2), j:j + 1], scale=SCALE,
                                            accum_out=st[0:rows, 2 * (u % 2) + 1, j:j + 1])
            last.then_inc(exp_ok, 1)

        for b in range(NSEQ):
            for pg in range(PAGES):
                n = 2 * b + pg
                act.wait_ge(*A.full(("ktr", b, pg, 0)))
                if n >= 2:
                    act.wait_ge(kt_free, n - 1)
                copy(KT[:, pg, 0:4, :], A.ap(("ktr", b, pg, 0))[:].rearrange("p (h s) -> p h s", h=4)).then_inc(a_act, 1)
            if b < NU:
                exps(b, P, len(unit_heads[b]), P * (unit_tile[b] + 1))
            if 1 <= b <= NU:
                u = b - 1
                act.wait_ge(*A.full(("pt", u)))
                if u >= 2:
                    act.wait_ge(*A.full(("o", u - 2)))
                copy(PT[:, u % 2, :], A.ap(("pt", u))[:]).then_inc(a_act, 1)
            if 2 <= b <= NU + 1:
                u = b - 2
                act.wait_ge(*A.full(("o", u)))
                hs, i = unit_heads[u], unit_tile[u]
                nh = len(hs)
                copy(hT[:, hs[0]:hs[0] + nh, P * i:P * i + P],
                     A.ap(("o", u))[:, 0:nh * P].rearrange("p (h t) -> p h t", h=nh)).then_inc(a_act, 1)
        act.wait_ge(*B.full("st"))
        act.wait_ge(stored, 16 * N_STORED)
        copy(stS, B.ap("st")[:]).then_inc(b_act, 1)
        act.wait_ge(*B.full("stn"))
        copy(stN, B.ap("stn")[0:NS, 0:H * NS]).then_inc(b_act, 1)
        for g in range(2):
            exps(NU + g, P, 1, PAST + NS)
        for g in range(2):
            act.wait_ge(*A.full(("spt", g)))
            copy(sPT[:, g, 0:2 * P], A.ap(("spt", g))[:, 0:2 * P])
            copy(sPT[0:NS, g, 2 * P:3 * P], A.ap(("spt", g))[0:NS, 2 * P:3 * P]).then_inc(a_act, 1)
        act.wait_ge(*B.full("so"))
        copy(hT[:, :, NP:T], B.ap("so")[:, 0:H * NS].rearrange("p (h q) -> p h q", h=H)).then_inc(b_act, 1)

        squares_and_root(1, A.freed(("wo", KD - 1)))
        act.wait_ge(stored, 16 * N_STORED)
        for f in range(NFB):
            act.wait_ge(*A.full(("fg", f)))
            if f >= 2:
                act.wait_ge(*A.freed(("fu", f - 2)))
            nc.scalar.activation(sg[:, f % 2, :], A.ap(("fg", f))[:, 0:T], ACT.Silu).then_inc(a_act, 1)

        act.wait_ge(*A.freed(("fd", KD - 1)))
        act.dma_start(wsr[:], a["gm_w_s"][0].rearrange("g i j -> i g j")).then_inc(ws_in, 16)
        act.dma_start(lng[:], a["gm_ln_g"][0:1, :].broadcast_to([P, D])).then_inc(gm_in, 16)
        act.dma_start(lnb[:], a["gm_ln_b"][0:1, :].broadcast_to([P, D])).then_inc(gm_in, 16)
        act.dma_start(bsb[:].rearrange("p g i -> p (g i)"),
                      a["gm_b_s"].rearrange("o g i -> o (g i)").broadcast_to([P, 8 * P])).then_inc(gm_in, 16)
        squares_and_root(2, A.freed(("fd", KD - 1)))
        for q in range(2):
            act.wait_ge(*A.full(("wst", q)))
            copy(wsT[:, 4 * q:4 * q + 4, :], A.ap(("wst", q))[:].rearrange("p (g i) -> p g i", g=4)).then_inc(a_act, 1)
        for half in range(2):
            for m in range(3):
                act.wait_ge(*A.full(("gv", m, half)))
                r = ROWS[m]
                nc.scalar.activation(gv[0:r, m, CH * half:CH * half + CH], A.ap(("gv", m, half))[0:r, :], ACT.Gelu)\
                  .then_inc(a_act, 1)
        for c in range(KD):
            act.wait_ge(*A.full(("gu", c)))
            nc.scalar.activation(gu[:, c, :], A.ap(("gu", c))[:, 0:T], ACT.Gelu).then_inc(a_act, 1)
        act.wait_ge(ln_ok, 1)
        nc.scalar.activation(mv[:, 0:2, 2:3], mv[:, 0:2, 1:2], ACT.Sqrt, bias=epst[:, 0:1])
        nc.scalar.activation(mv[0:NS, 2, 2:3], mv[0:NS, 2, 1:2], ACT.Sqrt, bias=epst[0:NS, 0:1]).then_inc(lnroot, 1)
        act.wait_ge(ln_ok, 4)
        store(o_gv, gv[0:NS, 2, :])

        squares_and_root(3, A.freed(("go", KD - 1)))
        act.wait_ge(stored, 16 * N_STORED)
        act.dma_start(wr[:], a["moe_w_router"][0].rearrange("(k p) e -> p k e", p=P)).then_inc(wr_in, 16)
        for m in range(3):
            for half in range(2):
                act.wait_ge(*A.full(("xo", m, half)))
                r = ROWS[m]
                copy(xtok[0:r, m, CH * half:CH * half + CH], A.ap(("xo", m, half))[0:r, :]).then_inc(a_act, 1)
        for m in range(3):
            act.wait_ge(neg_m1, m + 1)
            nc.scalar.activation(ex[0:ROWS[m], m, :], lg[0:ROWS[m], m, 0:E], ACT.Exp,
                                 bias=cden[0:ROWS[m], m, 0:1]).then_inc(ex_ok, 1)
        for m in range(3):
            for half in range(2):
                act.wait_ge(*A.full(("ho", m, half)))
                r = ROWS[m]
                copy(htok[0:r, m, CH * half:CH * half + CH], A.ap(("ho", m, half))[0:r, :]).then_inc(a_act, 1)

        def take_gathered(bank, half):
            return copy(xg[:, 4 * half:4 * half + 4, :], bank[:].rearrange("p (k s) -> p k s", k=4)).then_inc(xg_ok, 1)

        for half in range(2):
            act.wait_ge(ga_full, half + 1)
            take_gathered(banks[6 + half], half)
        act.wait_ge(items_ok, 1)
        n_items = act.value_load(cnt_i[0:1, 0:1], min_val=E, max_val=ITEMS)
        with act.Fori(0, n_items) as i:
            at = i * NCH + NCH
            def silu(c):
                act.wait_ge(g_full, at + (c + 1))
                if c == 0:
                    act.wait_ge(he_ok, at)
                elif c >= 2:
                    act.wait_ge(he_ok, at + (c - 1))
                nc.scalar.activation(sge[:, c % 2, :], banks[c % 2][:], ACT.Silu).then_inc(sg_ok, 1)

            def take_heT(c, bank):
                act.wait_ge(t_full, at + (c + 1))
                if c == 0:
                    act.wait_ge(d_used, at)
                elif c >= 2:
                    act.wait_ge(d_used, at + (c - 1))
                copy(heT[:, c % 2, :], bank[:]).then_inc(heT_ok, 1)

            silu(0)
            for c in range(1, NCH):
                silu(c)
                take_heT(c - 1, banks[6 + T_BANK[c - 1]])
                if c == 1:
                    act.wait_ge(pg_full, i + 2)
                    act.wait_ge(sc_full, i * 6 + 6)
                    copy(pgT[:], banks[7][:, 0:T]).then_inc(pgT_ok, 1)
            act.wait_ge(u_full, at + NCH)
            act.wait_ge(ga_full, i * 2 + 3)
            take_gathered(banks[7], 0)
            take_heT(NCH - 1, banks[6])
            act.wait_ge(ga_full, i * 2 + 4)
            take_gathered(banks[7], 1)
            act.wait_ge(d_used, at + NCH)
            for half in range(2):
                copy(ysb[:, CH * half:CH * half + CH], banks[4 + half][:]).then_inc(y_ok, 1)
        act.wait_ge(sc_ok, n_items * 6 + 12)
        for m in range(3):
            store(rows_of(o_y, m), xtok[0:ROWS[m], m, :])
        act.wait_ge(stored, 16 * N_STORED)

    @block.vector
    def _(dve):
        v = nc.vector
        done = [0]

        def link(ins):
            done[0] += 1
            ins.then_inc(chain, 1)
            dve.wait_ge(chain, done[0])

        def norm(n, xt_ready):
            if xt_ready:
                dve.wait_ge(*xt_ready)
            v.tensor_tensor(hT[:, 4:8, :], xT[:, 4:8, :], xT[:, 4:8, :], ALU.mult).then_inc(sq_dve, 1)
            dve.wait_ge(*B.freed(("ssq", n)))
            link(v.reciprocal(rt[:], rt[:]))
            for c in range(KD):
                v.scalar_tensor_tensor(out=hT[:, c, :], in0=xT[:, c, :], scalar=gT[:, 8 * n + c:8 * n + c + 1],
                                       in1=rt[:], op0=ALU.mult, op1=ALU.mult).then_inc(h_ready, 1)

        start_counters(dve, he_ok, sc_ok)
        dve.wait_ge(*A.full("par"))
        v.tensor_copy(gT[:], A.ap("par")[:, 0:35]).then_inc(a_dve, 1)
        for c in range(1, KD, 2):
            dve.wait_ge(*A.full(("xt", c)))
            v.tensor_copy(xT[:, c, :], A.ap(("xt", c))[:, 0:T]).then_inc(a_dve, 1)
        dve.wait_ge(*A.freed(("xt", KD - 1)))
        norm(0, A.freed(("xt", KD - 2)))
        dve.wait_ge(zeros, 1)
        for p in (1, 3):
            dve.wait_ge(*A.full(("qi", p)))
            bank = A.ap(("qi", p))
            for j in range(2):
                h, r = 2 * p + j, slice(ID * j, ID * j + ID)
                v.tensor_copy(qiz[r, h, :], bank[r, 0:T])
                last = v.tensor_copy(qix[r, :, h, :], bank[r, NP:T].rearrange("p (b t) -> p b t", t=TS))
            last.then_inc(a_dve, 1)
        dve.wait_ge(*B.freed("kissq"))
        link(v.reciprocal(rt[:], rt[:]))
        v.scalar_tensor_tensor(out=kiT[:], in0=A.ap("ki")[:, 0:T], scalar=gT[:, 34:35], in1=rt[:],
                               op0=ALU.mult, op1=ALU.mult).then_inc(a_dve, 1)
        dve.wait_ge(*A.full("wi"))
        v.tensor_scalar(wi[:], A.ap("wi")[:, 0:2 * IH].rearrange("p (m h) -> p m h", m=2), IH ** -0.5, None, ALU.mult)
        v.tensor_scalar(wiT[:], A.ap("wi")[0:IH, 64:64 + NS], IH ** -0.5, None, ALU.mult).then_inc(a_dve, 1)
        dve.wait_ge(const, 2)
        link(v.tensor_reduce(selm[:], selm4[:], AX.X, ALU.add))
        link(v.tensor_reduce(vmask[:], vmask3[:], AX.X, ALU.add))
        dve.wait_ge(*A.full("wrep"))
        v.tensor_tensor(selw[:, 0, :], selm[:, 0, :], A.ap("wrep")[:, 0:NS], ALU.mult)
        v.tensor_tensor(selw[:, 1, :], selm[:, 1, :], A.ap("wrep")[:, 0:NS], ALU.mult).then_inc(a_dve, 1)
        dve.wait_ge(*A.full("isel"))
        v.tensor_copy(scs[:], A.ap("isel")[0:NS, 0:WS]).then_inc(a_dve, 1)
        dve.wait_ge(*A.freed("isel"))
        link(v.tensor_tensor(scs[:, PAST:WS], scs[:, PAST:WS], vmask[:], ALU.mult))
        link(v.tensor_scalar(madd_t[:], vmask[:], 1.0, -NEG, ALU.subtract, ALU.mult))
        link(v.tensor_tensor(scs[:, PAST:WS], scs[:, PAST:WS], madd_t[:], ALU.add))
        for i, scx in ((0, sc0), (1, sc1)):
            w = P * (i + 1)
            per = CH // w
            for h in range(IH):
                g, j = (h // per, h % per) if i == 0 else (2 + h // per, h % per)
                if j == 0:
                    dve.wait_ge(*A.freed(("is", g)))
                src = rl[:, g, w * j:w * j + w]
                if h == 0:
                    ins = v.tensor_scalar(scx[:], src, wi[:, i, h:h + 1], None, ALU.mult)
                else:
                    ins = v.scalar_tensor_tensor(out=scx[:], in0=src, scalar=wi[:, i, h:h + 1], in1=scx[:],
                                                 op0=ALU.mult, op1=ALU.add)
                if h == IH - 1:
                    ins.then_inc(score_ok, 1)
                else:
                    link(ins)

        def rounds():
            for r in range(TOPK_S // 8 + 1):
                last = r == TOPK_S // 8
                link(v.max(m8[0:NS, :], scs[:]))
                if last:
                    link(v.memset(m8[0:NS, 1:8], MARK))
                link(v.match_replace(scs[:], m8[0:NS, :], scs[:], MARK))
                yield
            dve.wait_ge(masked, 1)
            for scx in (sc0, sc1):
                for r in range(TOPK_P // 8):
                    link(v.max(m8[:], scx[:]))
                    link(v.match_replace(scx[:], m8[:], scx[:], MARK))
                    yield
            v.tensor_scalar(sc0[:], sc0[:], MARKED, NEG, ALU.is_gt, ALU.mult).then_inc(smask_ok, 1)
            v.tensor_scalar(sc1[:], sc1[:], MARKED, NEG, ALU.is_gt, ALU.mult).then_inc(smask_ok, 1)
            link(v.tensor_scalar(scs[:], scs[:], MARKED, NEG, ALU.is_gt, ALU.mult))
            link(v.tensor_tensor(scs[:, PAST:WS], scs[:, PAST:WS], madd_t[:], ALU.min))
            v.tensor_copy(madd_s[:, 0:PAST], scs[:, 0:PAST])
            link(v.tensor_scalar(scs[:, PAST:WS], scs[:, PAST:WS], NEG, None, ALU.subtract))
            own = madd_s[:, PAST:PAST + NS].rearrange("p (b t) -> p b t", t=TS)
            link(v.tensor_tensor(own, scs[:, PAST:WS].unsqueeze(1).broadcast_to([NS, NSEQ, TS]),
                                 bmask[:].unsqueeze(2).broadcast_to([NS, NSEQ, TS]), ALU.mult))
            v.tensor_scalar(madd_s[:, PAST:PAST + NS], madd_s[:, PAST:PAST + NS], NEG, None, ALU.add).then_inc(mk_ok, 1)
            yield

        choosing = rounds()
        for n in range(16):
            dve.wait_ge(*B.freed(("qkn", n)))
            link(v.reciprocal(rt2[:, n % 2, :], rt2[:, n % 2, :]))
            dst, g = (qT, 32) if n < 8 else (kT, 33)
            v.scalar_tensor_tensor(out=dst[:, n % 8, :], in0=A.ap(("qk", n))[:, 0:T], scalar=gT[:, g:g + 1],
                                   in1=rt2[:, n % 2, :], op0=ALU.mult, op1=ALU.mult).then_inc(a_dve, 1)
            for _ in range(2):
                next(choosing, None)
        for _ in choosing:
            pass

        def softmax_in(u, rows, nh, w, bank, mask):
            half = sm[0:rows, u % 2, 0:nh * w].rearrange("p (h w) -> p h w", h=nh)
            if u >= 2:
                dve.wait_ge(*A.full(("pt", u - 2) if u - 2 < NU else ("spt", u - 2 - NU)))
            v.tensor_tensor(half, bank[0:rows, 0:nh * w].rearrange("p (h w) -> p h w", h=nh),
                            mask.unsqueeze(1).broadcast_to([rows, nh, w]), ALU.add).then_inc(a_dve, 1)
            return half

        def softmax_max(u, rows, nh, half, ready):
            dve.wait_ge(*ready)
            link(v.tensor_reduce(st[0:rows, 2 * (u % 2), 4:4 + nh], half, AX.X, ALU.max))
            v.tensor_scalar(st[0:rows, 2 * (u % 2), 0:nh], st[0:rows, 2 * (u % 2), 4:4 + nh], -SCALE, None, ALU.mult)\
             .then_inc(neg_ok, 1)

        def softmax_out(u, rows, nh, w, half):
            dve.wait_ge(exp_ok, u + 1)
            link(v.reciprocal(st[0:rows, 2 * (u % 2) + 1, 4:4 + nh], st[0:rows, 2 * (u % 2) + 1, 0:nh]))
            v.tensor_tensor(half, half, st[0:rows, 2 * (u % 2) + 1, 4:4 + nh].unsqueeze(2).broadcast_to([rows, nh, w]),
                            ALU.mult).then_inc(p_ok, 1)

        dve.wait_ge(masked, 2)
        for b in range(NSEQ):
            if b < NU:
                nh, w = len(unit_heads[b]), P * (unit_tile[b] + 1)
                dve.wait_ge(*A.full(("s", b)))
                half = softmax_in(b, P, nh, w, A.ap(("s", b)), (sc0, sc1)[unit_tile[b]][:])
                softmax_max(b, P, nh, half, A.freed(("s", b)))
            for pg in range(PAGES):
                n = 2 * b + pg
                dve.wait_ge(*A.full(("ktr", b, pg, 1)))
                if n >= 2:
                    dve.wait_ge(kt_free, n - 1)
                v.tensor_copy(KT[:, pg, 4:8, :], A.ap(("ktr", b, pg, 1))[:].rearrange("p (h s) -> p h s", h=4))\
                 .then_inc(a_dve, 1)
            if b < NU:
                softmax_out(b, P, nh, w, half)
        dve.wait_ge(*A.full("mrep"))
        v.tensor_copy(maddr[:], A.ap("mrep")[:, 0:PAST + NS]).then_inc(a_dve, 1)
        dve.wait_ge(*A.freed("mrep"))
        halves = []
        for g in range(2):
            dve.wait_ge(*A.full(("ss", g)))
            half = softmax_in(NU + g, P, 1, PAST + NS, A.ap(("ss", g)), maddr[:])
            softmax_max(NU + g, P, 1, half, A.freed(("ss", g)))
            halves.append(half)
        for g in range(2):
            softmax_out(NU + g, P, 1, PAST + NS, halves[g])

        def residual(name):
            for m in range(KD):
                dve.wait_ge(*A.full((name, m)))
                v.tensor_tensor(xT[:, m, :], xT[:, m, :], A.ap((name, m))[:, 0:T], ALU.add).then_inc(a_dve, 1)

        residual("wo")
        norm(1, A.freed(("wo", KD - 1)))
        dve.wait_ge(stored, 16 * 9)
        for f in range(NFB):
            dve.wait_ge(*A.full(("fu", f)))
            dve.wait_ge(*A.freed(("fg", f)))
            v.tensor_tensor(hh[:, f, :], sg[:, f % 2, :], A.ap(("fu", f))[:, 0:T], ALU.mult).then_inc(a_dve, 1)
        residual("fd")
        norm(2, A.freed(("fd", KD - 1)))

        dve.wait_ge(*A.full("wsr"))
        v.tensor_copy(wst4[:], A.ap("wsr")[0:NS, 0:8 * TS].rearrange("p (g i) -> p g i", g=8)).then_inc(a_dve, 1)
        dve.wait_ge(*A.freed("wsr"))
        for g in range(8):
            last = v.tensor_tensor(wsS[:, g, :].rearrange("p (b i) -> p b i", i=TS),
                                   wst4[:, g, :].unsqueeze(1).broadcast_to([NS, NSEQ, TS]),
                                   bmask[:].unsqueeze(2).broadcast_to([NS, NSEQ, TS]), ALU.mult)
        last.then_inc(wsS_ok, 1)
        for m in range(3):
            r = ROWS[m]
            for half in range(2):
                dve.wait_ge(*A.freed(("gv", m, half)))
                v.bn_stats(bn[0:r, m, 6 * half:6 * half + 6], gv[0:r, m, CH * half:CH * half + CH]).then_inc(ln_bad, 1)
            dve.wait_ge(ln_bad, 2 * m + 2)
            ins = v.bn_aggr(mv[0:r, m, 0:2], bn[0:r, m, :])
        ins.then_inc(ln_ok, 1)
        dve.wait_ge(lnroot, 1)
        link(v.reciprocal(mv[:, 0:2, 3:4], mv[:, 0:2, 2:3]))
        link(v.reciprocal(mv[0:NS, 2, 3:4], mv[0:NS, 2, 2:3]))
        dve.wait_ge(gm_in, 48)
        for m in range(3):
            r = ROWS[m]
            link(v.tensor_scalar(gv[0:r, m, :], gv[0:r, m, :], mv[0:r, m, 0:1], mv[0:r, m, 3:4],
                                 ALU.subtract, ALU.mult))
            link(v.tensor_tensor(gv[0:r, m, :], gv[0:r, m, :], lng[0:r, :], ALU.mult))
            v.tensor_tensor(gv[0:r, m, :], gv[0:r, m, :], lnb[0:r, :], ALU.add).then_inc(ln_ok, 1)
        for g in range(8):
            dve.wait_ge(*A.full(("mix", g)))
            bank = A.ap(("mix", g))
            v.tensor_tensor(hT[:, g, 0:NP].rearrange("p (c i) -> p c i", c=2),
                            bank[:, 0:NP].rearrange("p (c i) -> p c i", c=2),
                            bsb[:, g, :].unsqueeze(1).broadcast_to([P, 2, P]), ALU.add)
            v.tensor_tensor(hT[:, g, NP:T].rearrange("p (b i) -> p b i", i=TS),
                            bank[:, NP:T].rearrange("p (b i) -> p b i", i=TS),
                            bsb[:, g, 0:TS].unsqueeze(1).broadcast_to([P, NSEQ, TS]), ALU.add).then_inc(a_dve, 1)
            dve.wait_ge(*A.freed(("mix", g)))
            dve.wait_ge(*A.freed(("gu", g)))
            v.tensor_tensor(hT[:, g, :], hT[:, g, :], gu[:, g, :], ALU.mult).then_inc(mix_ok, 1)
        residual("go")
        norm(3, A.freed(("go", KD - 1)))

        dve.wait_ge(moe_zero, 1)
        dve.wait_ge(*A.full("rt"))
        v.tensor_copy(lg[:, 0:2, 0:E], A.ap("rt")[:, 0:2 * E].rearrange("p (m e) -> p m e", m=2))
        v.tensor_copy(lg[0:NS, 2, 0:E], A.ap("rt")[0:NS, 2 * E:3 * E]).then_inc(a_dve, 1)
        dve.wait_ge(*A.freed("rt"))
        for m in range(3):
            r = ROWS[m]
            link(v.max(r8[0:r, m, :], lg[0:r, m, 0:E]))
            v.tensor_scalar(cden[0:r, m, 0:1], r8[0:r, m, 0:1], -1.0, None, ALU.mult).then_inc(neg_m1, 1)
            link(v.tensor_copy(l8[0:r, m, 0:2], r8[0:r, m, 0:2]))
            link(v.match_replace(wk[0:r, m, :], l8[0:r, m, :], lg[0:r, m, :], MARK))
            ins = v.tensor_scalar(sel[0:r, m, :], wk[0:r, m, 0:E], MARKED, None, ALU.is_lt)
        ins.then_inc(sel_ok, 1)
        dve.wait_ge(sel_ok, 1)
        dve.wait_ge(ex_ok, 3)
        for m in range(3):
            r = ROWS[m]
            link(v.tensor_tensor(ex[0:r, m, :], ex[0:r, m, :], sel[0:r, m, :], ALU.mult))
            link(v.tensor_reduce(cden[0:r, m, 1:2], ex[0:r, m, :], AX.X, ALU.add))
            link(v.reciprocal(cden[0:r, m, 2:3], cden[0:r, m, 1:2]))
            for blk in range(MAXBLK):
                last = v.tensor_scalar(comb[0:r, m, E * blk:E * blk + E], ex[0:r, m, :], cden[0:r, m, 2:3], None, ALU.mult)
            link(last)
        dve.wait_ge(*A.full("pos"))
        v.tensor_copy(cnt[:, 0:E], A.ap("pos")[:, 3 * E:4 * E])
        v.tensor_copy(pos[:, 0:2, :], A.ap("pos")[:, 0:2 * E].rearrange("p (m e) -> p m e", m=2))
        v.tensor_copy(pos[0:NS, 2, :], A.ap("pos")[0:NS, 2 * E:3 * E]).then_inc(a_dve, 1)
        dve.wait_ge(*A.freed("pos"))
        for m in range(3):
            r = ROWS[m]
            link(v.scalar_tensor_tensor(out=pos[0:r, m, :], in0=pos[0:r, m, :], scalar=FAR, in1=sel[0:r, m, :],
                                        op0=ALU.add, op1=ALU.mult))
            for blk in range(MAXBLK):
                last = v.tensor_scalar(slot_of[0:r, m, E * blk:E * blk + E], pos[0:r, m, :], -FAR - P * blk, None, ALU.add)
            link(last)
        link(v.tensor_reduce(r8[0:1, 0, 0:1], cnt[0:1, 0:E], AX.X, ALU.max))
        link(v.tensor_scalar(r8[0:1, 0, 1:2], r8[0:1, 0, 0:1], float(P), float(E), ALU.is_gt, ALU.mult))
        link(v.tensor_scalar(r8[0:1, 0, 2:3], r8[0:1, 0, 0:1], float(2 * P), float(E), ALU.is_gt, ALU.mult))
        link(v.tensor_tensor(r8[0:1, 0, 3:4], r8[0:1, 0, 1:2], r8[0:1, 0, 2:3], ALU.add))
        v.tensor_scalar(cnt_i[0:1, 0:1], r8[0:1, 0, 3:4], float(E), None, ALU.add).then_inc(items_ok, 1)

        def picks(item, dst, gated):
            for m in range(3):
                r = ROWS[m]
                at = slot_of[0:r, m, bass.ds(item, 1)]
                if gated:
                    last = v.tensor_scalar(dst[0:r, m, :], iota[0:r, :], at, comb[0:r, m, bass.ds(item, 1)],
                                           ALU.is_equal, ALU.mult)
                else:
                    last = v.tensor_scalar(dst[0:r, m, :], iota[0:r, :], at, None, ALU.is_equal)
            return last

        picks(0, pick, False).then_inc(pick_ok, 1)
        dve.wait_ge(items_ok, 1)
        n_items = dve.value_load(cnt_i[0:1, 0:1], min_val=E, max_val=ITEMS)

        def add_back(first):
            for k in range(6):
                m, half = k // 2, k % 2
                dve.wait_ge(sc_full, first + (k + 1))
                x = xtok[0:ROWS[m], m, CH * half:CH * half + CH]
                v.tensor_tensor(x, x, banks[6 + k % 2][0:ROWS[m], :], ALU.add).then_inc(sc_ok, 1)

        with dve.Fori(0, n_items) as i:
            at = i * NCH + NCH
            dve.wait_ge(pg_full, i + 1)
            picks(i, pickg, True).then_inc(pickg_ok, 1)
            dve.wait_ge(sc_ok, i * 6 + 6)
            add_back(i * 6)
            for c in range(NCH):
                dve.wait_ge(u_full, at + (c + 1))
                dve.wait_ge(sg_ok, at + (c + 1))
                if c == 0:
                    dve.wait_ge(t_full, at)
                elif c >= 2:
                    dve.wait_ge(t_full, at + (c - 1))
                v.tensor_tensor(he[:, c % 2, :], sge[:, c % 2, :], banks[2 + c % 2][:], ALU.mult).then_inc(he_ok, 1)
                if c == 0:
                    dve.wait_ge(ga_full, i * 2 + 2)
                    picks(i + 1, pick, False).then_inc(pick_ok, 1)
        dve.wait_ge(sc_ok, n_items * 6 + 6)
        add_back(n_items * 6)

    @block.tensor
    def _(pe):
        mm = nc.tensor.matmul
        tr = nc.tensor.transpose

        def weights(name):
            pe.wait_ge(*arrived_at[name])

        def ssq(n):
            B.room(pe, ("ssq", n))
            pe.wait_ge(sq_act, n + 1)
            pe.wait_ge(sq_dve, n + 1)
            for c in range(KD):
                last = mm(B.ap(("ssq", n))[:, 0:T], ones[:], hT[:, c, :], start=(c == 0), stop=(c == KD - 1))
            last.then_inc(b_full, 1)

        def project(group, tile, col, ready, rhs=None, k=KD, width=P, ncols=T):
            A.room(pe, group)
            rhs = hT if rhs is None else rhs
            for c in range(k):
                if ready is not None:
                    pe.wait_ge(ready[0], ready[1] + c)
                last = mm(A.ap(group)[0:width, 0:ncols], tile[:, c, col:col + width], rhs[:, c, 0:ncols],
                          start=(c == 0), stop=(c == k - 1))
            last.then_inc(a_full, 1)

        def project_tokens(group, tile, m):
            A.room(pe, group)
            r = ROWS[m]
            for c in range(KD):
                last = mm(A.ap(group)[0:r, :], hT[:, c, P * m:P * m + r], tile[:, c, :],
                          start=(c == 0), stop=(c == KD - 1))
            last.then_inc(a_full, 1)

        def to_tokens(group, src, m, half, ready):
            A.room(pe, group)
            pe.wait_ge(*ready)
            r = ROWS[m]
            for j in range(4):
                last = tr(A.ap(group)[0:r, P * j:P * j + P], src[:, 4 * half + j, P * m:P * m + r], ident[:])
            last.then_inc(a_full, 1)

        start_counters(pe, g_full, u_full, d_used, t_full, pg_full)
        pe.wait_ge(const, 1)
        pe.wait_ge(par_in, 16 * 8)
        tr(A.ap("par")[:, 0:35], small[:], ident[0:35, 0:35]).then_inc(a_full, 1)
        for m in range(3):
            pe.wait_ge(x_in[m], 16)
        for c in range(KD):
            A.room(pe, ("xt", c))
            for m in range(3):
                r = ROWS[m]
                last = tr(A.ap(("xt", c))[:, P * m:P * m + r], tok[0:r, m, P * c:P * c + P], ident[0:r, 0:r])
            last.then_inc(a_full, 1)
        ssq(0)
        weights("qi")
        for p in range(4):
            project(("qi", p), w3("qi"), P * p, (h_ready, 1) if p == 0 else None)
        weights("kiwi")
        kw = w3("kiwi", SMALLW)
        project("ki", kw, 0, None)
        A.room(pe, "wi")
        for m in range(2):
            for c in range(KD):
                mm(A.ap("wi")[:, IH * m:IH * m + IH], hT[:, c, P * m:P * m + P], kw[:, c, 2 * ID:SMALLW],
                   start=(c == 0), stop=(c == KD - 1))
        for c in range(KD):
            last = mm(A.ap("wi")[0:IH, 64:64 + NS], kw[:, c, 2 * ID:SMALLW], hT[:, c, NP:T],
                      start=(c == 0), stop=(c == KD - 1))
        last.then_inc(a_full, 1)
        B.room(pe, "kissq")
        pe.wait_ge(kisq_ok, 1)
        mm(B.ap("kissq")[:, 0:T], ones[:], kisq[:], start=True, stop=True).then_inc(b_full, 1)
        A.room(pe, "wrep")
        pe.wait_ge(*A.freed("wi"))
        pe.wait_ge(const, 2)
        mm(A.ap("wrep")[:, 0:NS], rep8[:], wiT[:], start=True, stop=True).then_inc(a_full, 1)
        pe.wait_ge(kip2_ok, 1)
        for q in range(4):
            A.room(pe, ("kipt", q))
            for j in range(4):
                last = tr(A.ap(("kipt", q))[:, P * j:P * j + P],
                          kip[:, 4 * q + j, :, :].rearrange("p a d -> p (a d)"), ident[:])
            last.then_inc(a_full, 1)
        A.room(pe, "kio")
        pe.wait_ge(*A.freed("ki"))
        for m in range(3):
            last = tr(A.ap("kio")[0:ROWS[m], P * m:P * m + P], kiT[:, P * m:P * m + ROWS[m]], ident[:])
        last.then_inc(a_full, 1)
        pe.wait_ge(*A.freed(("qi", 2)))
        pe.wait_ge(*A.freed(("qi", 3)))
        for g in range(2):
            A.room(pe, ("iss", g))
            for j in range(4):
                b = 4 * g + j
                rows = A.ap(("iss", g))[NS * j:NS * j + NS, :]
                q = qix[:, b, :, :].rearrange("p h t -> p (h t)")
                pe.wait_ge(*A.freed(("kipt", b // 2)))
                mm(rows[:, 0:PAST], q, kipT[:, 2 * b:2 * b + 2, :].rearrange("p a s -> p (a s)"), start=True, stop=True)
                last = mm(rows[:, PAST:WS], q, kiT[:, NP + TS * b:NP + TS * b + TS], start=True, stop=True)
            last.then_inc(a_full, 1)
        A.room(pe, "isel")
        pe.wait_ge(*A.freed("wrep"))
        for g in range(2):
            pe.wait_ge(*A.freed(("iss", g)))
            last = mm(A.ap("isel")[0:NS, 0:WS], selw[:, g, :], rls[:, g, :], start=(g == 0), stop=(g == 1))
        last.then_inc(a_full, 1)
        for g in range(6):
            A.room(pe, ("is", g))
            i = 0 if g < 2 else 1
            w = P * (i + 1)
            per = CH // w
            for j in range(per):
                h = (g if i == 0 else g - 2) * per + j
                last = mm(A.ap(("is", g))[:, w * j:w * j + w], qiz[:, h, P * i:P * i + P], kiT[:, 0:w],
                          start=True, stop=True)
            last.then_inc(a_full, 1)

        def head_ssq(n):
            B.room(pe, ("qkn", n))
            pe.wait_ge(qsq, n + 1)
            mm(B.ap(("qkn", n))[:, 0:T], ones[:], sq2[:, n % 2, :], start=True, stop=True).then_inc(b_full, 1)

        for n in range(16):
            tile = (("q", "k")[n // 8], (n % 8) // 4)
            weights(tile)
            project(("qk", n), w3(tile), P * (n % 4), None)
            if n:
                head_ssq(n - 1)
        head_ssq(15)
        for half in range(2):
            weights(("v", half))
            for m in range(3):
                project_tokens(("v", m, half), w3(("v", half)), m)
        for m in range(3):
            for half in range(2):
                to_tokens(("kt", m, half), kT, m, half, A.freed(("qk", 15)))

        B.room(pe, "st")
        B.room(pe, "stn")
        for b in range(NSEQ):
            if b < NU:
                A.room(pe, ("s", b))
                w = P * (unit_tile[b] + 1)
                for j, h in enumerate(unit_heads[b]):
                    last = mm(A.ap(("s", b))[:, w * j:w * j + w], qT[:, h, P * unit_tile[b]:P * unit_tile[b] + P],
                              kT[:, h, 0:w], start=True, stop=True)
                last.then_inc(a_full, 1)
            weights(("kp", b // 2))
            for pg in range(PAGES):
                page = ring[:, slot[("kp", b // 2)], D * (2 * (b % 2) + pg):D * (2 * (b % 2) + pg) + D]
                for q in range(2):
                    A.room(pe, ("ktr", b, pg, q))
                    for j in range(4):
                        h = 4 * q + j
                        last = tr(A.ap(("ktr", b, pg, q))[:, P * j:P * j + P], page[:, P * h:P * h + P], ident[:])
                    last.then_inc(a_full, 1)
                pe.wait_ge(*A.freed(("ktr", b, pg, 0)))
                pe.wait_ge(*A.freed(("ktr", b, pg, 1)))
                for h in range(H):
                    c0 = H * NS * pg + NS * h + TS * b
                    last = mm(B.ap("st")[:, c0:c0 + TS], KT[:, pg, h, :], qT[:, h, NP + TS * b:NP + TS * b + TS],
                              start=True, stop=True)
                if (b, pg) == (NSEQ - 1, PAGES - 1):
                    last.then_inc(b_full, 1)
                else:
                    last.then_inc(kt_free, 1)
            if 1 <= b <= NU:
                u = b - 1
                A.room(pe, ("pt", u))
                pe.wait_ge(p_ok, u + 1)
                for j in range(4):
                    last = tr(A.ap(("pt", u))[:, P * j:P * j + P], sm[:, u % 2, P * j:P * j + P], ident[:])
                last.then_inc(a_full, 1)
            if 2 <= b <= NU + 1:
                u = b - 2
                A.room(pe, ("o", u))
                pe.wait_ge(*A.freed(("pt", u)))
                nk = unit_tile[u] + 1
                for j, h in enumerate(unit_heads[u]):
                    for kc in range(nk):
                        last = mm(A.ap(("o", u))[:, P * j:P * j + P], tok[:, kc, P * h:P * h + P],
                                  PT[:, u % 2, P * (nk * j + kc):P * (nk * j + kc) + P],
                                  start=(kc == 0), stop=(kc == nk - 1))
                last.then_inc(a_full, 1)
        for h in range(H):
            last = mm(B.ap("stn")[0:NS, NS * h:NS * h + NS], kT[:, h, NP:T], qT[:, h, NP:T], start=True, stop=True)
        last.then_inc(b_full, 1)
        A.room(pe, "mrep")
        pe.wait_ge(mk_ok, 1)
        mm(A.ap("mrep")[:, 0:PAST + NS], rep32[:], madd_s[:], start=True, stop=True).then_inc(a_full, 1)
        pe.wait_ge(*B.freed("stn"))
        for g in range(2):
            A.room(pe, ("ss", g))
            for pg in range(PAGES):
                tr(A.ap(("ss", g))[:, P * pg:P * pg + P], stS[:, H * NS * pg + P * g:H * NS * pg + P * g + P], ident[:])
            tr(A.ap(("ss", g))[:, PAST:PAST + NS], stN[:, P * g:P * g + P], ident[0:NS, 0:NS]).then_inc(a_full, 1)
        for g in range(2):
            A.room(pe, ("spt", g))
            pe.wait_ge(p_ok, NU + g + 1)
            s = sm[:, (NU + g) % 2, :]
            for pg in range(PAGES):
                tr(A.ap(("spt", g))[:, P * pg:P * pg + P], s[:, P * pg:P * pg + P], ident[:])
            tr(A.ap(("spt", g))[0:NS, PAST:PAST + P], s[:, PAST:PAST + NS], ident[:]).then_inc(a_full, 1)
        B.room(pe, "so")
        so = B.ap("so")
        pe.wait_ge(*A.freed(("spt", 1)))
        for h in range(H):
            g, j = h // 4, h % 4
            mm(so[:, NS * h:NS * h + NS], tok[0:NS, 2, P * h:P * h + P],
               sPT[0:NS, g, 2 * P + NS * j:2 * P + NS * j + NS], start=(h == 0), stop=False, skip_group_check=True)
        for b in range(NSEQ):
            weights(("vp", b // 2))
            for pg in range(PAGES):
                c0 = D * (2 * (b % 2) + pg)
                for h in range(H):
                    g, j = h // 4, h % 4
                    s0 = P * pg + NS * j + TS * b
                    last = mm(so[:, NS * h + TS * b:NS * h + TS * b + TS],
                              ring[:, slot[("vp", b // 2)], c0 + P * h:c0 + P * h + P], sPT[:, g, s0:s0 + TS],
                              start=False, stop=(b == NSEQ - 1 and pg == PAGES - 1 and h == H - 1),
                              skip_group_check=True)
            if b == NSEQ - 1:
                last.then_inc(b_full, 1)
            elif b % 2:
                last.then_inc(part_used, 1)
        for m in range(KD):
            weights(("wo", m // 4))
            if m == 0:
                pe.wait_ge(*A.freed(("o", NU - 1)))
                pe.wait_ge(*B.freed("so"))
            project(("wo", m), w3(("wo", m // 4)), P * (m % 4), None)

        ssq(1)
        for f in range(NFB):
            width = min(CH, DFF - CH * (f // 4))
            for k, name in enumerate(("fg", "fu")):
                weights((name, f // 4))
                project((name, f), w3((name, f // 4), width), P * (f % 4), (h_ready, KD + 1) if f == 0 and k == 0 else None)
        for half in range(2):
            for m in range(4):
                A.room(pe, ("fd", 4 * half + m))
            for part in range(3):
                weights(("fd", half, part))
                k = min(8, NFB - 8 * part)
                tile = w3(("fd", half, part), CH, k)
                for j in range(k):
                    f = 8 * part + j
                    if half == 0:
                        pe.wait_ge(*A.freed(("fu", f)))
                    for m in range(4):
                        last = mm(A.ap(("fd", 4 * half + m))[:, 0:T], tile[:, j, P * m:P * m + P], hh[:, f, :],
                                  start=(f == 0), stop=(f == NFB - 1))
                        if f == NFB - 1:
                            last.then_inc(a_full, 1)
                if part < 2:
                    last.then_inc(part_used, 1)

        ssq(2)
        pe.wait_ge(ws_in, 16)
        for q in range(2):
            A.room(pe, ("wst", q))
            for j in range(4):
                last = tr(A.ap(("wst", q))[:, P * j:P * j + P], wsr[:, 4 * q + j, :], ident[:])
            last.then_inc(a_full, 1)
        A.room(pe, "wsr")
        pe.wait_ge(ws_ok, 1)
        mm(A.ap("wsr")[0:NS, 0:8 * TS], rep4[:], wsT[0:TS, :, 0:TS], start=True, stop=True).then_inc(a_full, 1)
        pe.wait_ge(h_ready, 3 * KD)
        for half in range(2):
            weights(("gv", half))
            for m in range(3):
                project_tokens(("gv", m, half), w3(("gv", half)), m)
        for c in range(KD):
            weights(("gu", c // 4))
            project(("gu", c), w3(("gu", c // 4)), P * (c % 4), None)
        pe.wait_ge(ln_ok, 4)
        pe.wait_ge(wsS_ok, 1)
        for g in range(8):
            A.room(pe, ("mix", g))
            for m in range(3):
                r = ROWS[m]
                mat = wsT[:, g, :] if m < 2 else wsS[:, g, :]
                last = mm(A.ap(("mix", g))[:, P * m:P * m + r], gv[0:r, m, P * g:P * g + P], mat, start=True, stop=True)
            last.then_inc(a_full, 1)
        for m in range(KD):
            weights(("go", m // 4))
            project(("go", m), w3(("go", m // 4)), P * (m % 4), (mix_ok, 1) if m == 0 else None)

        ssq(3)
        for m in range(3):
            for half in range(2):
                to_tokens(("xo", m, half), xT, m, half, A.freed(("go", KD - 1)))
        A.room(pe, "rt")
        pe.wait_ge(h_ready, 4 * KD)
        pe.wait_ge(wr_in, 16)
        for m in range(3):
            r = ROWS[m]
            for c in range(KD):
                last = mm(A.ap("rt")[0:r, E * m:E * m + E], hT[:, c, P * m:P * m + r], wr[:, c, :],
                          start=(c == 0), stop=(c == KD - 1))
        last.then_inc(a_full, 1)
        for m in range(3):
            for half in range(2):
                to_tokens(("ho", m, half), hT, m, half, (h_ready, 4 * KD))
        A.room(pe, "pos")
        pe.wait_ge(sel_ok, 1)
        for m in range(4):
            r = ROWS[m] if m < 3 else P
            parts = list(range(min(m, 2) + 1)) if m < 3 else [0, 1, 2]
            for k in parts:
                kr = ROWS[k]
                left = upper[0:kr, 0:r] if k == m else ones[0:kr, 0:r]
                last = mm(A.ap("pos")[0:r, E * m:E * m + E], left, sel[0:kr, k, :], start=(k == 0), stop=(k == parts[-1]))
        last.then_inc(a_full, 1)

        def gather(half, bank):
            for j in range(4):
                c = 4 * half + j
                for m in range(3):
                    r = ROWS[m]
                    last = mm(bank[:, P * j:P * j + P], htok[0:r, m, P * c:P * c + P], pick[0:r, m, :],
                              start=(m == 0), stop=(m == 2))
            last.then_inc(ga_full, 1)

        def scatter(item6, waits):
            for k in range(6):
                m, half = k // 2, k % 2
                pe.wait_ge(*waits[k])
                r = ROWS[m]
                mm(banks[6 + k % 2][0:r, :], pgT[:, P * m:P * m + r], ysb[:, CH * half:CH * half + CH],
                   start=True, stop=True).then_inc(sc_full, 1)

        pe.wait_ge(*A.freed(("ho", 2, 1)))
        pe.wait_ge(pick_ok, 1)
        pe.wait_ge(*B.freed(("ssq", 3)))
        gather(0, banks[6])
        gather(1, banks[7])
        pe.wait_ge(moe_zero, 1)
        pe.wait_ge(*A.freed("pos"))
        pe.wait_ge(items_ok, 1)
        n_items = pe.value_load(cnt_i[0:1, 0:1], min_val=E, max_val=ITEMS)
        with pe.Fori(0, n_items) as i:
            at = i * NCH + NCH
            def gate_up(c, kind):
                sem_, val = expert_arrival(i, 3 * c + kind)
                pe.wait_ge(sem_, val)
                free = (sg_ok, he_ok)[kind]
                if c == 0:
                    pe.wait_ge(free, at)
                elif c >= 2:
                    pe.wait_ge(free, at + (c - 1))
                tile = tile_cols(expert_slot(3 * c + kind), CH)
                for k in range(KD):
                    last = mm(banks[2 * kind + c % 2][:], xg[:, k, :], tile[:, k, :], start=(k == 0), stop=(k == KD - 1))
                last.then_inc((g_full, u_full)[kind], 1)

            def turn(c, free):
                pe.wait_ge(he_ok, at + (c + 1))
                pe.wait_ge(*free)
                bank = banks[6 + T_BANK[c]]
                for j in range(4):
                    last = tr(bank[:, P * j:P * j + P], he[:, c % 2, P * j:P * j + P], ident[:])
                last.then_inc(t_full, 1)

            def down(c):
                sem_, val = expert_arrival(i, 3 * c + 2)
                pe.wait_ge(sem_, val)
                pe.wait_ge(heT_ok, at + (c + 1))
                if c == 0:
                    pe.wait_ge(y_ok, i * 2 + 2)
                tile = ring[:, expert_slot(3 * c + 2), :].rearrange("p (k f) -> p k f", k=CH // P)
                for j in range(CH // P):
                    for half in range(2):
                        last = mm(banks[4 + half][:], heT[:, c % 2, P * j:P * j + P],
                                  tile[:, j, CH * half:CH * half + CH],
                                  start=(c == 0 and j == 0), stop=(c == NCH - 1 and j == CH // P - 1))
                last.then_inc(d_used, 1)

            pe.wait_ge(xg_ok, i * 2 + 2)
            gate_up(0, 0)
            pe.wait_ge(y_ok, i * 2 + 2)
            pe.wait_ge(pgT_ok, i + 1)
            scatter(i * 6, [(heT_ok, at), (xg_ok, i * 2 + 2)] + [(sc_ok, i * 6 + (k + 5)) for k in range(2, 6)])
            gate_up(0, 1)
            for c in range(1, NCH):
                gate_up(c, 0)
                free = {0: (sc_ok, i * 6 + 11), 1: (heT_ok, at + 1), 2: (pgT_ok, i + 2)}
                turn(c - 1, free.get(c - 1, (heT_ok, at + (c - 2))))
                if c == 1:
                    pe.wait_ge(pickg_ok, i + 1)
                    pe.wait_ge(sc_ok, i * 6 + 12)
                    for m in range(3):
                        r = ROWS[m]
                        last = tr(banks[7][:, P * m:P * m + r], pickg[0:r, m, :], ident[0:r, 0:r])
                    last.then_inc(pg_full, 1)
                gate_up(c, 1)
                down(c - 1)
            pe.wait_ge(pick_ok, i + 2)
            pe.wait_ge(heT_ok, at + 5)
            gather(0, banks[7])
            turn(NCH - 1, (heT_ok, at + 6))
            pe.wait_ge(xg_ok, i * 2 + 3)
            gather(1, banks[7])
            down(NCH - 1)
        pe.wait_ge(y_ok, n_items * 2 + 2)
        pe.wait_ge(pgT_ok, n_items + 1)
        scatter(n_items * 6, [(heT_ok, n_items * NCH + NCH), (xg_ok, n_items * 2 + 2)]
                + [(sc_ok, n_items * 6 + (k + 5)) for k in range(2, 6)])

    return ctx


T_BANK = [0, 0, 1, 0, 1, 0, 0]


INS = ["x_prompt", "x_sample", "cache_k", "cache_v", "cache_kidx", "page_table", "norm_mix", "norm_ffn",
       "attn_w_in", "attn_g_q", "attn_g_k", "attn_g_kidx", "attn_w_out", "gm_w_in", "gm_ln_g", "gm_ln_b",
       "gm_w_s", "gm_b_s", "gm_w_out", "ffn_w_gate", "ffn_w_up", "ffn_w_down", "moe_w_router", "moe_w_gate",
       "moe_w_up", "moe_w_down"]
OUTS = {
    "y_prompt": (1, NP, D), "y_sample": (NSEQ, TS, D),
    "k_prompt": (1, NP // P, P, H, HD), "v_prompt": (1, NP // P, P, H, HD), "kidx_prompt": (1, NP // P, P, ID),
    "k_sample": (1, NSEQ, TS, H, HD), "v_sample": (1, NSEQ, TS, H, HD), "kidx_sample": (1, NSEQ, TS, ID),
    "gm_v_sample": (1, NSEQ, TS, D),
}


def kernel(**inputs):
    import numpy as np
    import concourse.bacc as bacc
    from concourse.bass_utils import run_bass_kernel_spmd

    nc = bacc.Bacc("TRN2", target_bir_lowering=False, num_devices=1)
    arrays, ins, outs = {}, {}, {}
    for name in INS:
        x = np.ascontiguousarray(inputs[name])
        arrays[f"in_{name}"] = x
        ins[name] = nc.dram_tensor(f"in_{name}", x.shape, mybir.dt.from_np(x.dtype), kind="ExternalInput").ap()
    for name, shape in OUTS.items():
        outs[name] = nc.dram_tensor(f"out_{name}", shape, F32, kind="ExternalOutput").ap()
    with build(nc, ins, outs):
        pass
    r = run_bass_kernel_spmd(nc, [arrays], core_ids=[0])
    return tuple(r.results[0][f"out_{name}"] for name in OUTS)
```

```python
from contextlib import ExitStack

import concourse.bass as bass
from concourse import mybir
from concourse.alu_op_type import AluOpType as ALU

F32 = mybir.dt.float32
F32R = mybir.dt.float32r
I32 = mybir.dt.int32
ACT = mybir.ActivationFunctionType
AX = mybir.AxisListType

P = 128
D = 1024
KD = D // P
NP = 256
NSEQ, TS = 8, 4
NS = NSEQ * TS
T = NP + NS
ROWS = [P, P, NS]
H, HD = 8, 128
IH, ID = 8, 64
PAST = 256
PAGES = PAST // P
WS = PAST + TS
TOPK_P, TOPK_S = 64, 65
DFF, DFE = 2816, 3584
NFB = DFF // P
E = 8
CH = 512
NCH = DFE // CH
SLOT = KD * CH
RING = 7
EPS = 1e-6
NEG = -1e30
MARK = -3e38
MARKED = -2e38
SCALE = HD ** -0.5
MAXBLK = (T + P - 1) // P
ITEMS = E * MAXBLK
FAR = 1000.0
QU = 4
WRING = 4
WD = 3
GATE, UP, DOWN = range(3)
TILES = [(GATE, 0), (UP, 0)]
for _c in range(1, NCH):
    TILES += [(GATE, _c), (UP, _c), (DOWN, _c - 1)]
TILES += [(DOWN, NCH - 1)]
PER_ITEM = len(TILES)
QI = PER_ITEM * QU


class Bank:

    def __init__(self, banks, full, freed):
        self.banks, self.full_sem, self.freed_sem = banks, full, freed
        self.order, self.index = [], {}

    def add(self, name, consumer):
        self.index[name] = len(self.order)
        self.order.append(consumer)

    def ap(self, name):
        return self.banks[self.index[name] % len(self.banks)]

    def full(self, name):
        return self.full_sem, self.index[name] + 1

    def freed(self, name):
        n = self.index[name]
        who = self.order[n]
        return self.freed_sem[who], self.order[:n + 1].count(who)

    def free_sem(self, name):
        return self.freed_sem[self.order[self.index[name]]]

    def room(self, engine, name):
        n = self.index[name] - len(self.banks)
        if n >= 0:
            who = self.order[n]
            engine.wait_ge(self.freed_sem[who], self.order[:n + 1].count(who))


def build(nc, a, out):
    ctx = ExitStack()

    def sem(name):
        return ctx.enter_context(nc.semaphore(name))

    def sb(name, shape, dt=F32, stack=None):
        return (stack or ctx).enter_context(nc.sbuf_tensor(name, shape, dt))

    def both(name, shape, stack=None):
        with ExitStack() as under:
            bits12 = sb(name + "_r", shape, F32R, stack=under)
        return sb(name, shape, stack=stack), bits12

    ring, ring_r = zip(*(both(f"ring{i}", [P, SLOT]) for i in range(RING)))
    ident = sb("ident", [P, P])
    ones = sb("ones", [P, P])
    upper = sb("upper", [P, P])
    iota = sb("iota", [P, P])
    epst = sb("epst", [P, 1])

    trunk = ExitStack()
    xT = sb("xT", [P, KD, T], stack=trunk)
    hT, hT_r = both("hT", [P, KD, T], trunk)
    bmask = sb("bmask", [NS, NSEQ], stack=trunk)
    rep4 = sb("rep4", [TS, NS], stack=trunk)
    gT = sb("gT", [P, 35], stack=trunk)
    rt = sb("rt", [P, T], stack=trunk)

    early = ExitStack()
    under = ExitStack()
    hE, hE_r = both("hE", [P, KD, T], under)
    under.close()
    tok = sb("tok", [P, 3, D], stack=early)
    vmask3 = sb("vmask3", [NS, TS, NSEQ], stack=early)
    vmask = sb("vmask", [NS, TS], stack=early)
    selm = sb("selm", [P, 2, NS], stack=early)
    rep32 = sb("rep32", [NS, P], stack=early)
    rep8 = sb("rep8", [IH, P], stack=early)
    small = sb("small", [35, P], stack=early)
    wi = sb("wi", [P, 2, IH], stack=early)
    wiT = sb("wiT", [IH, NS], stack=early)
    selw = sb("selw", [P, 2, NS], stack=early)
    kiT = sb("kiT", [P, T], stack=early)
    kitok = sb("kitok", [P, 3, ID], stack=early)
    sc0 = sb("sc0", [P, P], stack=early)
    sc1 = sb("sc1", [P, NP], stack=early)
    scs = sb("scs", [NS, WS], stack=early)
    m8 = sb("m8", [P, 8], stack=early)
    madd_s = sb("madd_s", [NS, PAST + NS], stack=early)
    madd_t = sb("madd_t", [NS, TS], stack=early)
    maddr = sb("maddr", [P, PAST + NS], stack=early)
    big = sb("big", [P, 6 * CH], stack=early)
    rl = big[:].rearrange("p (g c) -> p g c", g=6)
    ktok = big[:].rearrange("p (m c) -> p m c", m=3)
    stS = big[:, 0:CH]
    stN = big[0:NS, CH:CH + H * NS]
    sPT = big[:, 2 * CH:2 * CH + 6 * P].rearrange("p (g c) -> p g c", g=2)
    idx = ExitStack()
    qiz = sb("qiz", [P, IH, T], stack=idx)
    qix = sb("qix", [P, NSEQ, IH, TS], stack=idx)
    kip = sb("kip", [P, NSEQ * PAGES, 2, ID], stack=idx)
    kipT = sb("kipT", [P, NSEQ * PAGES, P], stack=idx)
    kip0 = sb("kip0", [P, NSEQ * PAGES, ID], stack=idx)
    kisq = sb("kisq", [P, T], stack=idx)
    rls = sb("rls", [P, 2, WS], stack=idx)
    selm4 = sb("selm4", [P, 2, NS, IH], stack=idx)
    idx.close()
    qT = sb("qT", [P, H, T], stack=early)
    kT = sb("kT", [P, H, T], stack=early)
    sq2 = sb("sq2", [P, 2, T], stack=early)
    rt2 = sb("rt2", [P, 2, T], stack=early)
    qkv = ExitStack()
    wde = sb("wde", [P, WRING, 1024], F32R, stack=qkv)
    qkv.close()
    KT = sb("KT", [P, 2, H, P], stack=early)
    sm = sb("sm", [P, 2, CH], stack=early)
    st = sb("st", [P, 4, 8], stack=early)
    PT = sb("PT", [P, 2, CH], stack=early)
    pt_i = sb("pt_i", [1, NSEQ * PAGES], I32, stack=early)
    early.close()

    dense = ExitStack()
    wd = sb("wd", [P, WD, 1024], F32R, stack=dense)
    hL, hL_r = both("hL", [P, KD, T], dense)

    ffn = ExitStack()
    hh = sb("hh", [P, NFB, T], F32R, stack=ffn)
    hhl, hhl_r = both("hhl", [P, NFB, T], ffn)
    sg = sb("sg", [P, 2, T], stack=ffn)
    ffn.close()

    gm = ExitStack()
    gv = sb("gv", [P, 3, D], stack=gm)
    gu = sb("gu", [P, KD, T], stack=gm)
    lng = sb("lng", [P, D], stack=gm)
    lnb = sb("lnb", [P, D], stack=gm)
    wsr = sb("wsr", [P, 8, P], stack=gm)
    wsT = sb("wsT", [P, 8, P], stack=gm)
    wsS = sb("wsS", [NS, 8, NS], stack=gm)
    wst4 = sb("wst4", [NS, 8, TS], stack=gm)
    bsb = sb("bsb", [P, 8, P], stack=gm)
    bn = sb("bn", [P, 3, 12], stack=gm)
    mv = sb("mv", [P, 3, 4], stack=gm)
    gm.close()
    dense.close()

    trunk.close()

    moe = ExitStack()
    wq = sb("wq", [P, WRING, 2, 1024], F32R, stack=moe)
    assert WRING * 2 * 1024 >= 2 * KD * T + 1024
    xtok = sb("xtok", [P, 3, D], stack=moe)
    htokh = sb("htokh", [P, 3, D], F32R, stack=moe)
    htokl = sb("htokl", [P, 3, D], F32R, stack=moe)
    sel = sb("sel", [P, 3, E], stack=moe)
    slot_of = sb("slot_of", [P, 3, ITEMS + 1], stack=moe)
    comb = sb("comb", [P, 3, ITEMS + 1], stack=moe)
    cnt_i = sb("cnt_i", [1, 1], I32, stack=moe)
    pick = sb("pick", [P, 3, P], F32R, stack=moe)
    pickT = sb("pickT", [P, 3 * P], F32R, stack=moe)
    xgh = sb("xgh", [P, KD, P], F32R, stack=moe)
    xgl = sb("xgl", [P, KD, P], F32R, stack=moe)
    ysbh = sb("ysbh", [P, D], F32R, stack=moe)
    ysbl = sb("ysbl", [P, D], F32R, stack=moe)
    heTh = sb("heTh", [P, CH], F32R, stack=moe)
    route = ExitStack()
    lg = sb("lg", [P, 3, 2 * E], stack=route)
    wk = sb("wk", [P, 3, 2 * E], stack=route)
    wr = sb("wr", [P, KD, E], stack=route)
    r8 = sb("r8", [P, 3, 8], stack=route)
    l8 = sb("l8", [P, 3, 8], stack=route)
    ex = sb("ex", [P, 3, E], stack=route)
    cden = sb("cden", [P, 3, 4], stack=route)
    pos = sb("pos", [P, 3, E], stack=route)
    cnt = sb("cnt", [P, 8], stack=route)
    route.close()
    heTl = sb("heTl", [P, CH], F32R, stack=moe)
    he = sb("he", [P, CH], stack=moe)
    moe.close()

    banks = [ctx.enter_context(nc.psum_tensor(f"bank{i}", [P, 512], F32)) for i in range(8)]

    a_full, a_act, a_dve = sem("a_full"), sem("a_act"), sem("a_dve")
    b_full, b_act, b_dve = sem("b_full"), sem("b_act"), sem("b_dve")
    A = Bank(banks[0:6], a_full, {"act": a_act, "dve": a_dve})
    B = Bank(banks[6:8], b_full, {"act": b_act, "dve": b_dve})
    w_in = [sem(f"w_in{i}") for i in range(RING)]
    x_in = [sem(f"x_in{i}") for i in range(3)]
    par_in, pt_in, kip_in, gm_in, wr_in, ws_in = (sem(n) for n in
        ("par_in", "pt_in", "kip_in", "gm_in", "wr_in", "ws_in"))
    const, zeros, chain, achain, pchain = (sem(n) for n in ("const", "zeros", "chain", "achain", "pchain"))
    sq_act, sq_dve, root, h_ready = (sem(n) for n in ("sq_act", "sq_dve", "root", "h_ready"))
    par_ok, kisq_ok, kiroot, kiT_ok, kip2_ok = (sem(n) for n in ("par_ok", "kisq_ok", "kiroot", "kiT_ok", "kip2_ok"))
    score_ok, masked, smask_ok, selw_ok = (sem(n) for n in ("score_ok", "masked", "smask_ok", "selw_ok"))
    qsq, qroot, qk_ok = (sem(n) for n in ("qsq", "qroot", "qk_ok"))
    neg_ok, exp_ok, p_ok = (sem(n) for n in ("neg_ok", "exp_ok", "p_ok"))
    kt_free, part_used = sem("kt_free"), sem("part_used")
    stored = sem("stored")
    ln_ok, lnroot, ws_ok, wsS_ok = (sem(n) for n in ("ln_ok", "lnroot", "ws_ok", "wsS_ok"))
    mk_ok, mix_ok, ln_bad = (sem(n) for n in ("mk_ok", "mix_ok", "ln_bad"))
    moe_zero, neg_m1, ex_ok, sel_ok, items_ok = (sem(n) for n in ("moe_zero", "neg_m1", "ex_ok", "sel_ok", "items_ok"))
    d_head, d_tail, p_tail, d_used = (sem(n) for n in ("d_head", "d_tail", "p_tail", "d_used"))
    h_head, h_tail, hh_head, hh_tail = (sem(n) for n in ("h_head", "h_tail", "hh_head", "hh_tail"))
    q_head, q_tail, q_used = sem("q_head"), sem("q_tail"), sem("q_used")
    t_full, pg_full, ga_full, sc_full = (sem(n) for n in ("t_full", "pg_full", "ga_full", "sc_full"))
    heTh_ok, xgh_ok, hoh_ok, yh_ok = (sem(n) for n in ("heTh_ok", "xgh_ok", "hoh_ok", "yh_ok"))
    sg_ok, he_ok, heT_ok, xg_ok, pickT_ok, y_ok, pick_ok, sc_ok = (sem(n) for n in
        ("sg_ok", "he_ok", "heT_ok", "xg_ok", "pickT_ok", "y_ok", "pick_ok", "sc_ok"))

    NU = 6
    unit_tile = [0, 0, 1, 1, 1, 1]
    unit_heads = [range(0, 4), range(4, 8), range(0, 2), range(2, 4), range(4, 6), range(6, 8)]
    A.add("par", "dve")
    for c in range(KD):
        A.add(("xt", c), "act" if c % 2 == 0 else "dve")
    B.add(("ssq", 0), "act")
    for p in range(4):
        A.add(("qi", p), "act" if p % 2 == 0 else "dve")
    A.add("ki", "dve")
    A.add("wi", "dve")
    B.add("kissq", "act")
    A.add("wrep", "dve")
    for q in range(4):
        A.add(("kipt", q), "act")
    A.add("kio", "act")
    for g in range(2):
        A.add(("iss", g), "act")
    A.add("isel", "dve")
    for g in range(6):
        A.add(("is", g), "act")
    for n in range(16):
        A.add(("qk", n), "dve")
        if n:
            B.add(("qkn", n - 1), "act")
    B.add(("qkn", 15), "act")
    for half in range(2):
        for m in range(3):
            A.add(("v", m, half), "act")
    for m in range(3):
        for half in range(2):
            A.add(("kt", m, half), "act")
    B.add("st", "act")
    B.add("stn", "act")
    NPG = NSEQ * PAGES
    A.add(("ktr", 0, 0), "act")
    A.add(("ktr", 0, 1), "dve")
    for b in range(NSEQ):
        if b < NU:
            A.add(("s", b), "dve")
        A.add(("ktr", 2 * b + 1, 0), "act")
        A.add(("ktr", 2 * b + 1, 1), "dve")
        if 1 <= b <= NU:
            A.add(("pt", b - 1), "act")
        if 2 * b + 2 < NPG:
            A.add(("ktr", 2 * b + 2, 0), "act")
            A.add(("ktr", 2 * b + 2, 1), "dve")
        if 2 <= b <= NU + 1:
            A.add(("o", b - 2), "act")
    A.add("mrep", "dve")
    for g in range(2):
        A.add(("ss", g), "dve")
    for g in range(2):
        A.add(("spt", g), "act")
    B.add("so", "act")
    for m in range(KD):
        A.add(("wo", m), "dve")
    B.add(("ssq", 1), "act")
    for f in range(NFB):
        A.add(("fg", f), "act")
        A.add(("fu", f), "dve")
    for m in range(KD):
        A.add(("fd", m), "dve")
    B.add(("ssq", 2), "act")
    for half in range(2):
        for m in range(3):
            A.add(("gv", m, half), "act")
    for q in range(2):
        A.add(("wst", q), "act")
    for c in range(KD):
        A.add(("gu", c), "act")
        if c == 1:
            A.add("wsr", "dve")
    for g in range(8):
        A.add(("mix", g), "dve")
    for m in range(KD):
        A.add(("go", m), "dve")
    B.add(("ssq", 3), "act")
    for m in range(3):
        for half in range(2):
            A.add(("xo", m, half), "act")
    A.add("rt", "dve")
    for m in range(3):
        for half in range(2):
            A.add(("ho", m, half), "dve")
    A.add("pos", "dve")

    def cols(w, c0, n):
        return w[:, c0:c0 + n].rearrange("(k p) f -> p k f", p=P)

    def tile_cols(slot, n):
        return ring[slot][:, 0:KD * n].rearrange("p (k f) -> p k f", k=KD)

    w_att, w_o = a["attn_w_in"][0], a["attn_w_out"][0]
    w_fg, w_fu, w_fd = a["ffn_w_gate"][0], a["ffn_w_up"][0], a["ffn_w_down"][0]
    w_gi, w_go = a["gm_w_in"][0], a["gm_w_out"][0]
    Q0, K0, V0, QI0 = 0, H * HD, 2 * H * HD, 3 * H * HD
    KI0 = QI0 + IH * ID
    WI0 = KI0 + ID
    SMALLW = 2 * ID + IH
    stream = [("qi", A.full(("qi", 3))), ("kiwi", A.full("wi"))]
    stream += [(("q", i), A.full(("qk", 4 * i + 3))) for i in range(2)]
    stream += [(("k", i), A.full(("qk", 8 + 4 * i + 3))) for i in range(2)]
    stream += [(("v", i), A.full(("v", 2, i))) for i in range(2)]
    stream += [(("kp", i), A.full(("ktr", 4 * i + 3, 1))) for i in range(4)]
    stream += [(("vp", i), (part_used, i + 1) if i < 3 else B.full("so")) for i in range(4)]
    stream += [(("wo", i), A.full(("wo", 4 * i + 3))) for i in range(2)]
    for i in range(6):
        last = min(4 * i + 3, NFB - 1)
        stream += [(("fg", i), A.full(("fg", last))), (("fu", i), A.full(("fu", last)))]
    for half in range(2):
        for part in range(3):
            over = (part_used, 3 + 2 * half + part + 1) if part < 2 else A.full(("fd", 4 * half + 3))
            stream += [(("fd", half, part), over)]
    stream += [(("gv", i), A.full(("gv", 2, i))) for i in range(2)]
    stream += [(("gu", i), A.full(("gu", 4 * i + 3))) for i in range(2)]
    stream += [(("go", i), A.full(("go", 4 * i + 3))) for i in range(2)]
    N0 = len(stream)
    slot, arrived_at, per_slot = {}, {}, [0] * RING
    for n, (name, _) in enumerate(stream):
        slot[name] = n % RING
        per_slot[n % RING] += 3 if name == "kiwi" else PAGES * 2 if name[0] in ("kp", "vp") else 1
        arrived_at[name] = (w_in[n % RING], 16 * per_slot[n % RING])
    base_count = list(per_slot)

    def w3(name, n=CH, k=KD, ring=ring):
        return ring[slot[name]][:, 0:k * n].rearrange("p (k f) -> p k f", k=k)

    quarters = [((("q", "k")[n // 8], (n % 8) // 4), "cols", n % 4) for n in range(16)]
    for half in range(2):
        quarters += [(("v", half), "rows", q) for q in range(QU)]
    F0 = len(quarters)
    for f in range(NFB):
        quarters += [(("fg", f // 4), "cols", f % 4), (("fu", f // 4), "cols", f % 4)]
    for half in range(2):
        for part in range(3):
            quarters += [(("fd", half, part), "rows", q) for q in range(min(8, NFB - 8 * part) // 2)]
    for half in range(2):
        quarters += [(("gv", half), "rows", q) for q in range(QU)]
    quarters += [(("gu", c // 4), "cols", c % 4) for c in range(KD)]
    quarters += [(("go", c // 4), "cols", c % 4) for c in range(KD)]
    first_of = {}
    for n, (tile, _, _) in enumerate(quarters):
        first_of.setdefault(tile, n)
    VQ0 = first_of["v", 0]
    FD0, GV0, GU0, GO0 = (first_of[t] for t in (("fd", 0, 0), ("gv", 0), ("gu", 0), ("go", 0)))

    def in_tile(n, ring=ring):
        tile, kind, q = quarters[n]
        if kind == "rows":
            return ring[slot[tile]][:, 1024 * q:1024 * q + 1024].rearrange("p (c f) -> p c f", c=2)
        width = min(CH, DFF - CH * tile[1]) if tile[0] in ("fg", "fu") else CH
        return w3(tile, width, ring=ring)[:, :, P * q:P * q + P]

    def its_tails_ready(n):
        return (p_tail, n + 1) if n < VQ0 else (d_tail, n - VQ0 + 1)

    def its_heads(n):
        buf = wde[:, n % WRING, :] if n < F0 else wd[:, (n - F0) % WD, :]
        return buf.rearrange("p (c f) -> p c f", c=2 if quarters[n][1] == "rows" else KD)

    def expert_slot(t):
        return (N0 + t) % RING

    def expert_arrival(i, t):
        s = expert_slot(t)
        return w_in[s], 16 * (base_count[s] + t // RING + 1) + i * (16 * 3)

    def after(i, kind, c):
        return q_used, i * QI + (QI + QU * (TILES.index((kind, c)) + 1))

    BASE = {q_used: QI, q_tail: QI, t_full: NCH, pg_full: 1, sg_ok: NCH, he_ok: NCH,
            heT_ok: NCH, pickT_ok: 1, y_ok: 2, sc_ok: 6}

    def start_counters(engine, *sems):
        for s in sems:
            engine.sem_inc(s, BASE[s])

    assert PER_ITEM == 3 * RING and QI % WRING == 0

    x_prompt, x_sample = a["x_prompt"][0], a["x_sample"].rearrange("b t d -> (b t) d")
    n_pool = a["cache_k"].shape[1]
    cache = {"kp": a["cache_k"][0].rearrange("n s h d -> n s (h d)"),
             "vp": a["cache_v"][0].rearrange("n s h d -> n s (h d)")}
    o_y = out["y_prompt"][0], out["y_sample"].rearrange("b t d -> (b t) d")
    o_k = (out["k_prompt"][0].rearrange("n s h d -> (n s) (h d)"),
           out["k_sample"][0].rearrange("b t h d -> (b t) (h d)"))
    o_v = (out["v_prompt"][0].rearrange("n s h d -> (n s) (h d)"),
           out["v_sample"][0].rearrange("b t h d -> (b t) (h d)"))
    o_ki = (out["kidx_prompt"][0].rearrange("n s d -> (n s) d"),
            out["kidx_sample"][0].rearrange("b t d -> (b t) d"))
    o_gv = out["gm_v_sample"][0].rearrange("b t d -> (b t) d")
    N_STORED = 0

    def rows_of(pair, m):
        return pair[0][P * m:P * m + P, :] if m < 2 else pair[1]

    block = ctx.enter_context(nc.Block())

    @block.sync
    def _(sp):
        sp.dma_start(pt_i[0:1, :], a["page_table"].rearrange("(o b) n -> o (b n)", o=1)).then_inc(pt_in, 16)
        for m in range(1, 3):
            src = x_prompt[P * m:P * m + P, :] if m < 2 else x_sample
            sp.dma_start(tok[0:ROWS[m], m, :], src).then_inc(x_in[m], 16)
        pages = None
        for n, (name, _) in enumerate(stream):
            if n >= RING:
                sp.wait_ge(*stream[n - RING][1])
            if n == 1:
                sp.wait_ge(par_in, 16 * 8)
            if n == 3:
                sp.wait_ge(kip_in, 16 * NSEQ * PAGES)
            s, got = n % RING, w_in[n % RING]
            if name == "qi":
                sp.dma_start(tile_cols(s, CH), cols(w_att, QI0, CH)).then_inc(got, 16)
            elif name == "kiwi":
                t = tile_cols(s, SMALLW)
                sp.dma_start(t[:, :, 0:ID], cols(w_att, KI0, ID)).then_inc(got, 16)
                sp.dma_start(t[:, :, ID:2 * ID], cols(w_att, KI0, ID)).then_inc(got, 16)
                sp.dma_start(t[:, :, 2 * ID:SMALLW], cols(w_att, WI0, IH)).then_inc(got, 16)
            elif name[0] in ("q", "k", "v"):
                c0 = {"q": Q0, "k": K0, "v": V0}[name[0]] + CH * name[1]
                sp.dma_start(tile_cols(s, CH), cols(w_att, c0, CH)).then_inc(got, 16)
            elif name[0] in ("kp", "vp"):
                if pages is None:
                    sp.wait_ge(pt_in, 16)
                    pages = True
                for j in range(2 * PAGES):
                    pg = sp.value_load(pt_i[0:1, 4 * name[1] + j:4 * name[1] + j + 1], min_val=0, max_val=n_pool - 1)
                    src = cache[name[0]][bass.ds(pg, 1), :, :].rearrange("o s c -> (o s) c")
                    sp.dma_start(ring[s][:, D * j:D * j + D], src).then_inc(got, 16)
            elif name[0] == "wo":
                sp.dma_start(tile_cols(s, CH), cols(w_o, CH * name[1], CH)).then_inc(got, 16)
            elif name[0] in ("fg", "fu"):
                w = w_fg if name[0] == "fg" else w_fu
                width = min(CH, DFF - CH * name[1])
                sp.dma_start(tile_cols(s, width), cols(w, CH * name[1], width)).then_inc(got, 16)
            elif name[0] == "fd":
                _, half, part = name
                k = min(8, NFB - 8 * part)
                src = w_fd[1024 * part:1024 * part + P * k, CH * half:CH * half + CH]
                sp.dma_start(ring[s][:, 0:k * CH].rearrange("p (k f) -> p k f", k=k),
                             src.rearrange("(k p) f -> p k f", p=P)).then_inc(got, 16)
            elif name[0] in ("gv", "gu"):
                c0 = (D if name[0] == "gv" else 0) + CH * name[1]
                sp.dma_start(tile_cols(s, CH), cols(w_gi, c0, CH)).then_inc(got, 16)
            elif name[0] == "go":
                sp.dma_start(tile_cols(s, CH), cols(w_go, CH * name[1], CH)).then_inc(got, 16)

        def expert_tile(e, t):
            s, (kind, c) = expert_slot(t), TILES[t]
            if kind != DOWN:
                w = a["moe_w_gate" if kind == GATE else "moe_w_up"][0]
                src = w[bass.ds(e, 1), :, CH * c:CH * c + CH].rearrange("o (k p) f -> p (o k) f", p=P)
                sp.dma_start(tile_cols(s, CH), src).then_inc(w_in[s], 16)
            else:
                src = a["moe_w_down"][0][bass.ds(e, 1), CH * c:CH * c + CH, :]
                sp.dma_start(ring[s][:].rearrange("p (k f) -> p k f", k=CH // P),
                             src.rearrange("o (k p) f -> p (o k) f", p=P)).then_inc(w_in[s], 16)

        for t in range(PER_ITEM):
            if t < RING:
                sp.wait_ge(*stream[N0 + t - RING][1])
            else:
                sp.wait_ge(q_tail, QI + QU * (t - RING + 1))
            expert_tile(0, t)
        sp.wait_ge(q_tail, QI + QU * (PER_ITEM - RING + 1))
        expert_tile(1, 0)
        sp.wait_ge(items_ok, 1)
        n_items = sp.value_load(cnt_i[0:1, 0:1], min_val=E, max_val=ITEMS)
        with sp.Fori(1, n_items) as i:
            for t in range(1, PER_ITEM + 1):
                sp.wait_ge(q_tail, i * QI + (QI + QU * (t - RING + 1)))
                expert_tile((i + t // PER_ITEM) % E, t % PER_ITEM)

    @block.gpsimd
    def _(pool):
        done = [0]

        def link(ins):
            done[0] += 1
            ins.then_inc(pchain, 1)
            pool.wait_ge(pchain, done[0])

        def memsets(*pairs):
            for t, v in pairs:
                last = nc.gpsimd.memset(t, v)
            link(last)

        def select(t, op, fill, base, pattern, cm):
            return nc.gpsimd.affine_select(out=t, in_=t, compare_op=op, fill=fill, base=base, pattern=pattern,
                                           channel_multiplier=cm)

        memsets((ident[:], 0.0), (ones[:], 1.0), (epst[:], EPS))
        select(ident[:], ALU.not_equal, 1.0, 0, [[-1, P]], 1).then_inc(const, 1)
        for t in (qiz, qix):
            last = nc.gpsimd.memset(t[:], 0.0)
        last.then_inc(zeros, 1)
        memsets((rep8[:], 0.0), (selm4[:], 0.0), (rep32[:], 0.0), (rep4[:], 0.0), (bmask[:], 1.0),
                (vmask3[:], 1.0), (upper[:], 1.0))
        select(rep8[:].rearrange("k (j h t) -> k j h t", j=4, h=IH), ALU.not_equal, 1.0, 0,
               [[0, 4], [-1, IH], [0, TS]], 1)
        for g in range(2):
            select(selm4[:, g, :, :].rearrange("p (b t) h -> p b t h", t=TS), ALU.not_equal, 1.0, P * g,
                   [[-NS, NSEQ], [-1, TS], [-TS, IH]], 1)
        select(rep32[:].rearrange("k (j q) -> k j q", j=4), ALU.not_equal, 1.0, 0, [[0, 4], [-1, NS]], 1)
        select(rep4[:].rearrange("k (b t) -> k b t", t=TS), ALU.not_equal, 1.0, 0, [[0, NSEQ], [-1, TS]], 1)
        select(upper[:], ALU.is_ge, 0.0, -1, [[1, P]], -1)
        select(bmask[:], ALU.is_ge, 0.0, 0, [[-TS, NSEQ]], 1)
        link(select(vmask3[:], ALU.is_ge, 0.0, 0, [[-1, TS], [-TS, NSEQ]], 1))
        select(bmask[:], ALU.is_ge, 0.0, TS - 1, [[TS, NSEQ]], -1)
        select(vmask3[:], ALU.is_ge, 0.0, TS - 1, [[0, TS], [TS, NSEQ]], -1)
        nc.gpsimd.iota(iota[:], [[1, P]], base=0, channel_multiplier=0,
                       allow_small_or_imprecise_dtypes=True).then_inc(const, 1)
        pool.wait_ge(kip_in, 16 * NSEQ * PAGES)
        for j in range(2):
            last = nc.gpsimd.tensor_copy(kip[:, :, j, :], kip0[:, :, :])
        last.then_inc(kip2_ok, 1)
        def tail_of(n):
            pool.wait_ge(d_head, n + 1)
            nc.gpsimd.tensor_tensor(in_tile(n, ring_r), in_tile(n), its_heads(n).bitcast(F32), ALU.subtract)\
              .then_inc(p_tail, 1)

        pool.wait_ge(*A.full("wi"))
        for c in range(KD):
            pool.wait_ge(h_head, c + 1)
            nc.gpsimd.tensor_tensor(hE_r[:, c, :], hE[:, c, :], hT_r[:, c, :].bitcast(F32), ALU.subtract)\
              .then_inc(h_tail, 1)
        for n in range(7):
            tail_of(n)
        pool.wait_ge(score_ok, 2)
        select(sc0[:], ALU.is_ge, NEG, 0, [[-1, P]], 1)
        select(sc1[:], ALU.is_ge, NEG, P, [[-1, NP]], 1).then_inc(masked, 1)
        for n in range(7, VQ0):
            tail_of(n)
        pool.wait_ge(smask_ok, 2)
        select(sc0[:], ALU.is_ge, NEG, 0, [[-1, P]], 1)
        select(sc1[:], ALU.is_ge, NEG, P, [[-1, NP]], 1).then_inc(masked, 1)
        pool.wait_ge(*A.freed(("wst", 1)))
        select(wsT[:], ALU.is_ge, 0.0, 0, [[0, 8], [1, P]], -1).then_inc(ws_ok, 1)
        pool.wait_ge(*A.freed(("go", KD - 1)))
        for t, v in ((slot_of, -FAR), (comb, 0.0), (lg, MARK), (l8, MARK), (pickT, 0.0), (ysbh, 0.0), (ysbl, 0.0)):
            last = nc.gpsimd.memset(t[:] if t.dtype == F32 else t[:].bitcast(F32), v)
        last.then_inc(moe_zero, 1)

    @block.scalar
    def _(act):
        nonlocal N_STORED
        done = [0]

        def link(ins):
            done[0] += 1
            ins.then_inc(achain, 1)
            act.wait_ge(achain, done[0])

        def copy(dst, src):
            return nc.scalar.activation(dst, src, ACT.Copy)

        def store(dst, src):
            nonlocal N_STORED
            N_STORED += 1
            act.dma_start(dst, src).then_inc(stored, 16)

        split = [0]

        def heads_before(stop):
            while split[0] < stop:
                n = split[0]
                act.wait_ge(*arrived_at[quarters[n][0]])
                ahead, first = (WRING, 0) if n < F0 else (WD, F0)
                if n >= first + ahead:
                    act.wait_ge(d_used, n - ahead + 1)
                copy(its_heads(n), in_tile(n)).then_inc(d_head, 1)
                split[0] += 1

        def h_heads(ready, seen, src=hL):
            for c in range(KD):
                act.wait_ge(ready, seen + c + 1)
                copy(hT_r[:, c, :], src[:, c, :]).then_inc(h_head, 1)

        start_counters(act, sg_ok, pickT_ok)
        act.dma_start(tok[:, 0, :], x_prompt[0:P, :]).then_inc(x_in[0], 16)
        for r, w in enumerate((a["norm_mix"][0], a["norm_ffn"][0], a["norm_mix"][1], a["norm_ffn"][1])):
            act.dma_start(small[8 * r:8 * r + 8, :], w.rearrange("(c p) -> c p", p=P)).then_inc(par_in, 16)
        act.dma_start(small[32:33, :], a["attn_g_q"]).then_inc(par_in, 16)
        act.dma_start(small[33:34, :], a["attn_g_k"]).then_inc(par_in, 16)
        act.dma_start(small[34:35, 0:ID], a["attn_g_kidx"]).then_inc(par_in, 16)
        act.dma_start(small[34:35, ID:P], a["attn_g_kidx"]).then_inc(par_in, 16)
        act.wait_ge(pt_in, 16)
        for j in range(NSEQ * PAGES):
            pg = act.value_load(pt_i[0:1, j:j + 1], min_val=0, max_val=n_pool - 1)
            act.dma_start(kip0[:, j, :], a["cache_kidx"][0][bass.ds(pg, 1), :, :].rearrange("o s d -> (o s) d"))\
               .then_inc(kip_in, 16)

        def squares_and_root(n, xt_ready):
            act.wait_ge(*xt_ready)
            nc.scalar.activation(hT[:, 0:4, :], xT[:, 0:4, :], ACT.Square).then_inc(sq_act, 1)
            act.wait_ge(*B.full(("ssq", n)))
            nc.scalar.activation(rt[:], B.ap(("ssq", n))[:, 0:T], ACT.Sqrt, bias=epst[:, 0:1], scale=1.0 / D)\
              .then_inc(b_act, 1)

        for c in range(0, KD, 2):
            act.wait_ge(*A.full(("xt", c)))
            copy(xT[:, c, :], A.ap(("xt", c))[:, 0:T]).then_inc(a_act, 1)
        act.wait_ge(const, 1)
        act.wait_ge(*A.freed(("xt", KD - 2)))
        squares_and_root(0, A.freed(("xt", KD - 1)))
        act.wait_ge(zeros, 1)
        for p in (0, 2):
            act.wait_ge(*A.full(("qi", p)))
            bank = A.ap(("qi", p))
            for j in range(2):
                h, r = 2 * p + j, slice(ID * j, ID * j + ID)
                copy(qiz[r, h, :], bank[r, 0:T])
                last = copy(qix[r, :, h, :], bank[r, NP:T].rearrange("p (b t) -> p b t", t=TS))
            last.then_inc(a_act, 1)
        act.wait_ge(*A.full("ki"))
        nc.scalar.activation(kisq[:], A.ap("ki")[:, 0:T], ACT.Square).then_inc(kisq_ok, 1)
        act.wait_ge(*B.full("kissq"))
        act.wait_ge(h_ready, KD)
        nc.scalar.activation(rt[:], B.ap("kissq")[:, 0:T], ACT.Sqrt, bias=epst[:, 0:1], scale=1.0 / P)\
          .then_inc(b_act, 1)
        for q in range(4):
            act.wait_ge(*A.full(("kipt", q)))
            copy(kipT[:, 4 * q:4 * q + 4, :], A.ap(("kipt", q))[:].rearrange("p (a s) -> p a s", a=4)).then_inc(a_act, 1)
        act.wait_ge(*A.full("kio"))
        kio = A.ap("kio")[:, 0:3 * P].rearrange("p (m d) -> p m d", m=3)
        copy(kitok[:, 0:2, :], kio[:, 0:2, 0:ID])
        copy(kitok[0:NS, 2, :], kio[0:NS, 2, 0:ID]).then_inc(a_act, 1)
        act.wait_ge(*A.freed("kio"))
        for m in range(3):
            store(rows_of(o_ki, m), kitok[0:ROWS[m], m, :])
        for g in range(2):
            act.wait_ge(*A.full(("iss", g)))
            nc.scalar.activation(rls[:, g, :], A.ap(("iss", g))[:, 0:WS], ACT.Relu, scale=ID ** -0.5).then_inc(a_act, 1)
        h_heads(h_ready, 0, hE)
        act.wait_ge(*A.full("isel"))
        for g in range(6):
            if g < WRING:
                heads_before(g + 1)
            act.wait_ge(*A.full(("is", g)))
            nc.scalar.activation(rl[:, g, :], A.ap(("is", g))[:], ACT.Relu, scale=ID ** -0.5).then_inc(a_act, 1)
        for n in range(17):
            if n < 16:
                act.wait_ge(*A.full(("qk", n)))
                if n >= 2:
                    act.wait_ge(*B.full(("qkn", n - 2)))
                nc.scalar.activation(sq2[:, n % 2, :], A.ap(("qk", n))[:, 0:T], ACT.Square).then_inc(qsq, 1)
                heads_before(n + 1 + WRING)
            if n >= 1:
                j = n - 1
                act.wait_ge(*B.full(("qkn", j)))
                if j >= 2:
                    act.wait_ge(*A.freed(("qk", j - 2)))
                nc.scalar.activation(rt2[:, j % 2, :], B.ap(("qkn", j))[:, 0:T], ACT.Sqrt, bias=epst[:, 0:1],
                                     scale=1.0 / HD).then_inc(b_act, 1)
        heads_before(F0)
        act.wait_ge(*A.full(("v", 2, 1)))
        for half in range(2):
            for m in range(3):
                r = ROWS[m]
                copy(tok[0:r, m, CH * half:CH * half + CH], A.ap(("v", m, half))[0:r, :]).then_inc(a_act, 1)
        act.wait_ge(*A.freed(("v", 2, 1)))
        for m in range(3):
            store(rows_of(o_v, m), tok[0:ROWS[m], m, :])
        for m in range(3):
            for half in range(2):
                act.wait_ge(*A.full(("kt", m, half)))
                r = ROWS[m]
                copy(ktok[0:r, m, CH * half:CH * half + CH], A.ap(("kt", m, half))[0:r, :]).then_inc(a_act, 1)
        act.wait_ge(*A.freed(("kt", 2, 1)))
        for m in range(3):
            store(rows_of(o_k, m), ktok[0:ROWS[m], m, :])

        def exps(u, rows, nh, w):
            act.wait_ge(neg_ok, u + 1)
            for j in range(nh):
                last = nc.scalar.activation(sm[0:rows, u % 2, w * j:w * j + w], sm[0:rows, u % 2, w * j:w * j + w],
                                            ACT.Exp, bias=st[0:rows, 2 * (u % 2), j:j + 1], scale=SCALE,
                                            accum_out=st[0:rows, 2 * (u % 2) + 1, j:j + 1])
            last.then_inc(exp_ok, 1)

        def take_kt(n):
            act.wait_ge(*A.full(("ktr", n, 0)))
            if n >= 2:
                act.wait_ge(kt_free, n - 1)
            copy(KT[:, n % 2, 0:4, :], A.ap(("ktr", n, 0))[:].rearrange("p (h s) -> p h s", h=4)).then_inc(a_act, 1)

        take_kt(0)
        for b in range(NSEQ):
            take_kt(2 * b + 1)
            if b < NU:
                exps(b, P, len(unit_heads[b]), P * (unit_tile[b] + 1))
            if 1 <= b <= NU:
                u = b - 1
                act.wait_ge(*A.full(("pt", u)))
                if u >= 2:
                    act.wait_ge(*A.full(("o", u - 2)))
                copy(PT[:, u % 2, :], A.ap(("pt", u))[:]).then_inc(a_act, 1)
            if 2 * b + 2 < NPG:
                take_kt(2 * b + 2)
            if 2 <= b <= NU + 1:
                u = b - 2
                act.wait_ge(*A.full(("o", u)))
                hs, i = unit_heads[u], unit_tile[u]
                nh = len(hs)
                copy(hT[:, hs[0]:hs[0] + nh, P * i:P * i + P],
                     A.ap(("o", u))[:, 0:nh * P].rearrange("p (h t) -> p h t", h=nh)).then_inc(a_act, 1)
        act.wait_ge(*B.full("st"))
        act.wait_ge(stored, 16 * N_STORED)
        copy(stS, B.ap("st")[:]).then_inc(b_act, 1)
        act.wait_ge(*B.full("stn"))
        copy(stN, B.ap("stn")[0:NS, 0:H * NS]).then_inc(b_act, 1)
        for g in range(2):
            exps(NU + g, P, 1, PAST + NS)
        for g in range(2):
            act.wait_ge(*A.full(("spt", g)))
            copy(sPT[:, g, 0:2 * P], A.ap(("spt", g))[:, 0:2 * P])
            copy(sPT[0:NS, g, 2 * P:3 * P], A.ap(("spt", g))[0:NS, 2 * P:3 * P]).then_inc(a_act, 1)
        act.wait_ge(*B.full("so"))
        copy(hT[:, :, NP:T], B.ap("so")[:, 0:H * NS].rearrange("p (h q) -> p h q", h=H)).then_inc(b_act, 1)

        def hidden_head(f):
            act.wait_ge(*A.freed(("fu", f)))
            copy(hh[:, f, :], hhl[:, f, :]).then_inc(hh_head, 1)

        act.wait_ge(stored, 16 * N_STORED)
        heads_before(F0 + WD)
        squares_and_root(1, A.freed(("wo", KD - 1)))
        h_heads(h_ready, KD)
        for f in range(NFB):
            act.wait_ge(*A.full(("fg", f)))
            if f >= 2:
                act.wait_ge(*A.freed(("fu", f - 2)))
            nc.scalar.activation(sg[:, f % 2, :], A.ap(("fg", f))[:, 0:T], ACT.Silu).then_inc(a_act, 1)
            heads_before(F0 + 2 * f + 1 + WD)
            if f >= 1:
                hidden_head(f - 1)
            heads_before(F0 + 2 * f + 2 + WD)
        hidden_head(NFB - 1)
        heads_before(GV0 + WD)

        act.wait_ge(*A.freed(("fd", KD - 1)))
        act.dma_start(wsr[:], a["gm_w_s"][0].rearrange("g i j -> i g j")).then_inc(ws_in, 16)
        act.dma_start(lng[:], a["gm_ln_g"][0:1, :].broadcast_to([P, D])).then_inc(gm_in, 16)
        act.dma_start(lnb[:], a["gm_ln_b"][0:1, :].broadcast_to([P, D])).then_inc(gm_in, 16)
        act.dma_start(bsb[:].rearrange("p g i -> p (g i)"),
                      a["gm_b_s"].rearrange("o g i -> o (g i)").broadcast_to([P, 8 * P])).then_inc(gm_in, 16)
        squares_and_root(2, A.freed(("fd", KD - 1)))
        h_heads(h_ready, 2 * KD)
        for half in range(2):
            heads_before(GV0 + QU * half + QU + WD)
            for m in range(3):
                act.wait_ge(*A.full(("gv", m, half)))
                r = ROWS[m]
                nc.scalar.activation(gv[0:r, m, CH * half:CH * half + CH], A.ap(("gv", m, half))[0:r, :], ACT.Gelu)\
                  .then_inc(a_act, 1)
        for q in range(2):
            act.wait_ge(*A.full(("wst", q)))
            copy(wsT[:, 4 * q:4 * q + 4, :], A.ap(("wst", q))[:].rearrange("p (g i) -> p g i", g=4)).then_inc(a_act, 1)
        for c in range(KD):
            heads_before(GU0 + c + 1 + WD)
            act.wait_ge(*A.full(("gu", c)))
            nc.scalar.activation(gu[:, c, :], A.ap(("gu", c))[:, 0:T], ACT.Gelu).then_inc(a_act, 1)
            if c == 2:
                act.wait_ge(ln_ok, 1)
                nc.scalar.activation(mv[:, 0:2, 2:3], mv[:, 0:2, 1:2], ACT.Sqrt, bias=epst[:, 0:1])
                nc.scalar.activation(mv[0:NS, 2, 2:3], mv[0:NS, 2, 1:2], ACT.Sqrt, bias=epst[0:NS, 0:1]).then_inc(lnroot, 1)
        act.wait_ge(ln_ok, 4)
        store(o_gv, gv[0:NS, 2, :])
        h_heads(mix_ok, 0)
        heads_before(GO0 + KD)

        squares_and_root(3, A.freed(("go", KD - 1)))
        act.wait_ge(stored, 16 * N_STORED)
        act.dma_start(wr[:], a["moe_w_router"][0].rearrange("(k p) e -> p k e", p=P)).then_inc(wr_in, 16)
        for m in range(3):
            for half in range(2):
                act.wait_ge(*A.full(("xo", m, half)))
                r = ROWS[m]
                copy(xtok[0:r, m, CH * half:CH * half + CH], A.ap(("xo", m, half))[0:r, :]).then_inc(a_act, 1)
        for m in range(3):
            act.wait_ge(neg_m1, m + 1)
            nc.scalar.activation(ex[0:ROWS[m], m, :], lg[0:ROWS[m], m, 0:E], ACT.Exp,
                                 bias=cden[0:ROWS[m], m, 0:1]).then_inc(ex_ok, 1)
        for m in range(3):
            for half in range(2):
                act.wait_ge(*A.full(("ho", m, half)))
                r = ROWS[m]
                copy(htokh[0:r, m, CH * half:CH * half + CH], A.ap(("ho", m, half))[0:r, :]).then_inc(hoh_ok, 1)

        def take_gathered(bank, half):
            return copy(xgh[:, 4 * half:4 * half + 4, :], bank[:].rearrange("p (k s) -> p k s", k=4)).then_inc(xgh_ok, 1)

        def heads(i, t):
            for q in range(QU):
                if q == 0:
                    act.wait_ge(*expert_arrival(i, t))
                act.wait_ge(q_used, i * QI + (QI + QU * t + q - WRING + 1))
                copy(wq[:, (QU * t + q) % WRING, 0, :], ring[expert_slot(t)][:, 1024 * q:1024 * q + 1024])\
                    .then_inc(q_head, 1)

        act.wait_ge(*A.freed("pos"))
        heads(0, 0)
        for half in range(2):
            act.wait_ge(ga_full, half + 1)
            take_gathered(banks[6 + half], half)
        act.wait_ge(items_ok, 1)
        n_items = act.value_load(cnt_i[0:1, 0:1], min_val=E, max_val=ITEMS)
        with act.Fori(0, n_items) as i:
            at = i * NCH + NCH

            def silu(c):
                act.wait_ge(*after(i, GATE, c))
                act.wait_ge(t_full, at + c if c else at)
                nc.scalar.activation(he[:], banks[c % 2][:], ACT.Silu).then_inc(sg_ok, 1)

            def take_heT(c):
                act.wait_ge(t_full, at + (c + 1))
                if c:
                    act.wait_ge(*after(i, DOWN, c - 1))
                copy(heTh[:], banks[6 + T_BANK[c]][:]).then_inc(heTh_ok, 1)

            for t in range(1, PER_ITEM):
                heads(i, t)
                kind, c = TILES[t]
                if kind == UP:
                    if c >= 1:
                        take_heT(c - 1)
                    silu(c)
                    if c == 1:
                        act.wait_ge(pg_full, i + 2)
                        act.wait_ge(sc_full, i * 6 + 6)
                        copy(pickT[:, 0:T], banks[7][:, 0:T]).then_inc(pickT_ok, 1)
            act.wait_ge(*after(i, UP, NCH - 1))
            act.wait_ge(ga_full, i * 2 + 3)
            take_gathered(banks[7], 0)
            take_heT(NCH - 1)
            act.wait_ge(ga_full, i * 2 + 4)
            take_gathered(banks[7], 1)
            heads(i + 1, 0)
            act.wait_ge(*after(i, DOWN, NCH - 1))
            for half in range(2):
                copy(ysbh[:, CH * half:CH * half + CH], banks[4 + half][:]).then_inc(yh_ok, 1)
        act.wait_ge(*expert_arrival(n_items, 0))
        act.wait_ge(sc_ok, n_items * 6 + 12)
        for m in range(3):
            store(rows_of(o_y, m), xtok[0:ROWS[m], m, :])
        act.wait_ge(stored, 16 * N_STORED)

    @block.vector
    def _(dve):
        v = nc.vector
        done = [0]

        def link(ins):
            done[0] += 1
            ins.then_inc(chain, 1)
            dve.wait_ge(chain, done[0])

        split, turned = [VQ0], [KD]

        def tails_before(stop):
            while split[0] < stop:
                n = split[0]
                dve.wait_ge(d_head, n + 1)
                v.tensor_tensor(in_tile(n, ring_r), in_tile(n), its_heads(n).bitcast(F32), ALU.subtract)\
                 .then_inc(d_tail, 1)
                split[0] += 1

        def h_tail_of(c):
            turned[0] += 1
            dve.wait_ge(h_head, turned[0])
            v.tensor_tensor(hL_r[:, c, :], hL[:, c, :], hT_r[:, c, :].bitcast(F32), ALU.subtract).then_inc(h_tail, 1)

        def norm(n, xt_ready, dst=None):
            if xt_ready:
                dve.wait_ge(*xt_ready)
            v.tensor_tensor(hT[:, 4:8, :], xT[:, 4:8, :], xT[:, 4:8, :], ALU.mult).then_inc(sq_dve, 1)
            dve.wait_ge(*B.freed(("ssq", n)))
            link(v.reciprocal(rt[:], rt[:]))
            for c in range(KD):
                v.scalar_tensor_tensor(out=(hT if dst is None else dst)[:, c, :], in0=xT[:, c, :],
                                       scalar=gT[:, 8 * n + c:8 * n + c + 1],
                                       in1=rt[:], op0=ALU.mult, op1=ALU.mult).then_inc(h_ready, 1)
                if dst is hL and c >= 1:
                    h_tail_of(c - 1)
            if dst is hL:
                h_tail_of(KD - 1)

        start_counters(dve, he_ok, sc_ok, heT_ok, q_tail, y_ok)
        dve.wait_ge(*A.full("par"))
        v.tensor_copy(gT[:], A.ap("par")[:, 0:35]).then_inc(a_dve, 1)
        for c in range(1, KD, 2):
            dve.wait_ge(*A.full(("xt", c)))
            v.tensor_copy(xT[:, c, :], A.ap(("xt", c))[:, 0:T]).then_inc(a_dve, 1)
        dve.wait_ge(*A.freed(("xt", KD - 1)))
        dve.wait_ge(*A.full(("xt", KD - 1)))
        norm(0, A.freed(("xt", KD - 2)), hE)
        dve.wait_ge(zeros, 1)
        for p in (1, 3):
            dve.wait_ge(*A.full(("qi", p)))
            bank = A.ap(("qi", p))
            for j in range(2):
                h, r = 2 * p + j, slice(ID * j, ID * j + ID)
                v.tensor_copy(qiz[r, h, :], bank[r, 0:T])
                last = v.tensor_copy(qix[r, :, h, :], bank[r, NP:T].rearrange("p (b t) -> p b t", t=TS))
            last.then_inc(a_dve, 1)
        dve.wait_ge(*B.freed("kissq"))
        link(v.reciprocal(rt[:], rt[:]))
        v.scalar_tensor_tensor(out=kiT[:], in0=A.ap("ki")[:, 0:T], scalar=gT[:, 34:35], in1=rt[:],
                               op0=ALU.mult, op1=ALU.mult).then_inc(a_dve, 1)
        dve.wait_ge(*A.full("wi"))
        v.tensor_scalar(wi[:], A.ap("wi")[:, 0:2 * IH].rearrange("p (m h) -> p m h", m=2), IH ** -0.5, None, ALU.mult)
        v.tensor_scalar(wiT[:], A.ap("wi")[0:IH, 64:64 + NS], IH ** -0.5, None, ALU.mult).then_inc(a_dve, 1)
        dve.wait_ge(const, 2)
        link(v.tensor_reduce(selm[:], selm4[:], AX.X, ALU.add))
        link(v.tensor_reduce(vmask[:], vmask3[:], AX.X, ALU.add))
        dve.wait_ge(*A.full("wrep"))
        v.tensor_tensor(selw[:, 0, :], selm[:, 0, :], A.ap("wrep")[:, 0:NS], ALU.mult)
        v.tensor_tensor(selw[:, 1, :], selm[:, 1, :], A.ap("wrep")[:, 0:NS], ALU.mult).then_inc(a_dve, 1)
        dve.wait_ge(*A.full("isel"))
        v.tensor_copy(scs[:], A.ap("isel")[0:NS, 0:WS]).then_inc(a_dve, 1)
        dve.wait_ge(*A.freed("isel"))
        link(v.tensor_tensor(scs[:, PAST:WS], scs[:, PAST:WS], vmask[:], ALU.mult))
        link(v.tensor_scalar(madd_t[:], vmask[:], 1.0, -NEG, ALU.subtract, ALU.mult))
        link(v.tensor_tensor(scs[:, PAST:WS], scs[:, PAST:WS], madd_t[:], ALU.add))
        for i, scx in ((0, sc0), (1, sc1)):
            w = P * (i + 1)
            per = CH // w
            for h in range(IH):
                g, j = (h // per, h % per) if i == 0 else (2 + h // per, h % per)
                if j == 0:
                    dve.wait_ge(*A.freed(("is", g)))
                src = rl[:, g, w * j:w * j + w]
                if h == 0:
                    ins = v.tensor_scalar(scx[:], src, wi[:, i, h:h + 1], None, ALU.mult)
                else:
                    ins = v.scalar_tensor_tensor(out=scx[:], in0=src, scalar=wi[:, i, h:h + 1], in1=scx[:],
                                                 op0=ALU.mult, op1=ALU.add)
                if h == IH - 1:
                    ins.then_inc(score_ok, 1)
                else:
                    link(ins)

        def rounds():
            for r in range(TOPK_S // 8 + 1):
                last = r == TOPK_S // 8
                link(v.max(m8[0:NS, :], scs[:]))
                if last:
                    link(v.memset(m8[0:NS, 1:8], MARK))
                link(v.match_replace(scs[:], m8[0:NS, :], scs[:], MARK))
                yield
            dve.wait_ge(masked, 1)
            for scx in (sc0, sc1):
                for r in range(TOPK_P // 8):
                    link(v.max(m8[:], scx[:]))
                    link(v.match_replace(scx[:], m8[:], scx[:], MARK))
                    yield
            v.tensor_scalar(sc0[:], sc0[:], MARKED, NEG, ALU.is_gt, ALU.mult).then_inc(smask_ok, 1)
            v.tensor_scalar(sc1[:], sc1[:], MARKED, NEG, ALU.is_gt, ALU.mult).then_inc(smask_ok, 1)
            link(v.tensor_scalar(scs[:], scs[:], MARKED, NEG, ALU.is_gt, ALU.mult))
            link(v.tensor_tensor(scs[:, PAST:WS], scs[:, PAST:WS], madd_t[:], ALU.min))
            v.tensor_copy(madd_s[:, 0:PAST], scs[:, 0:PAST])
            link(v.tensor_scalar(scs[:, PAST:WS], scs[:, PAST:WS], NEG, None, ALU.subtract))
            own = madd_s[:, PAST:PAST + NS].rearrange("p (b t) -> p b t", t=TS)
            link(v.tensor_tensor(own, scs[:, PAST:WS].unsqueeze(1).broadcast_to([NS, NSEQ, TS]),
                                 bmask[:].unsqueeze(2).broadcast_to([NS, NSEQ, TS]), ALU.mult))
            v.tensor_scalar(madd_s[:, PAST:PAST + NS], madd_s[:, PAST:PAST + NS], NEG, None, ALU.add).then_inc(mk_ok, 1)
            yield

        choosing = rounds()
        for n in range(16):
            dve.wait_ge(*B.freed(("qkn", n)))
            link(v.reciprocal(rt2[:, n % 2, :], rt2[:, n % 2, :]))
            dst, g = (qT, 32) if n < 8 else (kT, 33)
            v.scalar_tensor_tensor(out=dst[:, n % 8, :], in0=A.ap(("qk", n))[:, 0:T], scalar=gT[:, g:g + 1],
                                   in1=rt2[:, n % 2, :], op0=ALU.mult, op1=ALU.mult).then_inc(a_dve, 1)
            if n + WRING >= VQ0:
                tails_before(n + 1 + WRING)
            next(choosing, None)
        for n in range(VQ0 + WRING, F0):
            tails_before(n + 1)
            for _ in range(3):
                next(choosing, None)
        for _ in choosing:
            pass

        def softmax_in(u, rows, nh, w, bank, mask):
            half = sm[0:rows, u % 2, 0:nh * w].rearrange("p (h w) -> p h w", h=nh)
            if u >= 2:
                dve.wait_ge(*A.full(("pt", u - 2) if u - 2 < NU else ("spt", u - 2 - NU)))
            v.tensor_tensor(half, bank[0:rows, 0:nh * w].rearrange("p (h w) -> p h w", h=nh),
                            mask.unsqueeze(1).broadcast_to([rows, nh, w]), ALU.add).then_inc(a_dve, 1)
            return half

        def softmax_max(u, rows, nh, half, ready):
            dve.wait_ge(*ready)
            link(v.tensor_reduce(st[0:rows, 2 * (u % 2), 4:4 + nh], half, AX.X, ALU.max))
            v.tensor_scalar(st[0:rows, 2 * (u % 2), 0:nh], st[0:rows, 2 * (u % 2), 4:4 + nh], -SCALE, None, ALU.mult)\
             .then_inc(neg_ok, 1)

        def softmax_out(u, rows, nh, w, half):
            dve.wait_ge(exp_ok, u + 1)
            link(v.reciprocal(st[0:rows, 2 * (u % 2) + 1, 4:4 + nh], st[0:rows, 2 * (u % 2) + 1, 0:nh]))
            v.tensor_tensor(half, half, st[0:rows, 2 * (u % 2) + 1, 4:4 + nh].unsqueeze(2).broadcast_to([rows, nh, w]),
                            ALU.mult).then_inc(p_ok, 1)

        def take_kt(n):
            dve.wait_ge(*A.full(("ktr", n, 1)))
            if n >= 2:
                dve.wait_ge(kt_free, n - 1)
            v.tensor_copy(KT[:, n % 2, 4:8, :], A.ap(("ktr", n, 1))[:].rearrange("p (h s) -> p h s", h=4))\
             .then_inc(a_dve, 1)

        take_kt(0)
        dve.wait_ge(masked, 2)
        for b in range(NSEQ):
            if b < NU:
                nh, w = len(unit_heads[b]), P * (unit_tile[b] + 1)
                dve.wait_ge(*A.full(("s", b)))
                half = softmax_in(b, P, nh, w, A.ap(("s", b)), (sc0, sc1)[unit_tile[b]][:])
                softmax_max(b, P, nh, half, A.freed(("s", b)))
            take_kt(2 * b + 1)
            if b < NU:
                softmax_out(b, P, nh, w, half)
            if 2 * b + 2 < NPG:
                take_kt(2 * b + 2)
        dve.wait_ge(*A.full("mrep"))
        v.tensor_copy(maddr[:], A.ap("mrep")[:, 0:PAST + NS]).then_inc(a_dve, 1)
        dve.wait_ge(*A.freed("mrep"))
        halves = []
        for g in range(2):
            dve.wait_ge(*A.full(("ss", g)))
            half = softmax_in(NU + g, P, 1, PAST + NS, A.ap(("ss", g)), maddr[:])
            softmax_max(NU + g, P, 1, half, A.freed(("ss", g)))
            halves.append(half)
        for g in range(2):
            softmax_out(NU + g, P, 1, PAST + NS, halves[g])

        def residual(name, m):
            dve.wait_ge(*A.full((name, m)))
            v.tensor_tensor(xT[:, m, :], xT[:, m, :], A.ap((name, m))[:, 0:T], ALU.add).then_inc(a_dve, 1)

        dve.wait_ge(stored, 16 * 9)
        tails_before(F0 + WD)
        for m in range(KD):
            residual("wo", m)
        norm(1, A.freed(("wo", KD - 1)), hL)

        def hidden_tail(f):
            dve.wait_ge(hh_head, f + 1)
            v.tensor_tensor(hhl_r[:, f, :], hhl[:, f, :], hh[:, f, :].bitcast(F32), ALU.subtract)\
             .then_inc(hh_tail, 1)

        for f in range(NFB):
            tails_before(F0 + 2 * f + 1 + WD)
            dve.wait_ge(*A.full(("fu", f)))
            dve.wait_ge(*A.freed(("fg", f)))
            v.tensor_tensor(hhl[:, f, :], sg[:, f % 2, :], A.ap(("fu", f))[:, 0:T], ALU.mult).then_inc(a_dve, 1)
            if f >= 1:
                hidden_tail(f - 1)
            tails_before(F0 + 2 * f + 2 + WD)
        hidden_tail(NFB - 1)
        tails_before(first_of["fd", 1, 0] + WD)
        for m in range(KD):
            residual("fd", m)
            if m == 3:
                tails_before(GV0 + WD)
        norm(2, A.freed(("fd", KD - 1)), hL)

        tails_before(GU0 + WD)
        for m in range(3):
            if m:
                tails_before(GU0 + WD + m)
            r = ROWS[m]
            for half in range(2):
                dve.wait_ge(*A.freed(("gv", m, half)))
                v.bn_stats(bn[0:r, m, 6 * half:6 * half + 6], gv[0:r, m, CH * half:CH * half + CH]).then_inc(ln_bad, 1)
            dve.wait_ge(ln_bad, 2 * m + 2)
            ins = v.bn_aggr(mv[0:r, m, 0:2], bn[0:r, m, :])
        ins.then_inc(ln_ok, 1)
        dve.wait_ge(*A.full("wsr"))
        v.tensor_copy(wst4[:], A.ap("wsr")[0:NS, 0:8 * TS].rearrange("p (g i) -> p g i", g=8)).then_inc(a_dve, 1)
        dve.wait_ge(*A.freed("wsr"))
        for g in range(8):
            last = v.tensor_tensor(wsS[:, g, :].rearrange("p (b i) -> p b i", i=TS),
                                   wst4[:, g, :].unsqueeze(1).broadcast_to([NS, NSEQ, TS]),
                                   bmask[:].unsqueeze(2).broadcast_to([NS, NSEQ, TS]), ALU.mult)
        last.then_inc(wsS_ok, 1)
        dve.wait_ge(lnroot, 1)
        link(v.reciprocal(mv[:, 0:2, 3:4], mv[:, 0:2, 2:3]))
        link(v.reciprocal(mv[0:NS, 2, 3:4], mv[0:NS, 2, 2:3]))
        dve.wait_ge(gm_in, 48)
        for m in range(3):
            r = ROWS[m]
            link(v.tensor_scalar(gv[0:r, m, :], gv[0:r, m, :], mv[0:r, m, 0:1], mv[0:r, m, 3:4],
                                 ALU.subtract, ALU.mult))
            link(v.tensor_tensor(gv[0:r, m, :], gv[0:r, m, :], lng[0:r, :], ALU.mult))
            v.tensor_tensor(gv[0:r, m, :], gv[0:r, m, :], lnb[0:r, :], ALU.add).then_inc(ln_ok, 1)
            tails_before(GU0 + WD + 3 + m)
        tails_before(GO0 + WD)
        for g in range(8):
            dve.wait_ge(*A.full(("mix", g)))
            bank = A.ap(("mix", g))
            v.tensor_tensor(hL[:, g, 0:NP].rearrange("p (c i) -> p c i", c=2),
                            bank[:, 0:NP].rearrange("p (c i) -> p c i", c=2),
                            bsb[:, g, :].unsqueeze(1).broadcast_to([P, 2, P]), ALU.add)
            v.tensor_tensor(hL[:, g, NP:T].rearrange("p (b i) -> p b i", i=TS),
                            bank[:, NP:T].rearrange("p (b i) -> p b i", i=TS),
                            bsb[:, g, 0:TS].unsqueeze(1).broadcast_to([P, NSEQ, TS]), ALU.add).then_inc(a_dve, 1)
            dve.wait_ge(*A.freed(("mix", g)))
            dve.wait_ge(*A.freed(("gu", g)))
            v.tensor_tensor(hL[:, g, :], hL[:, g, :], gu[:, g, :], ALU.mult).then_inc(mix_ok, 1)
            if g:
                h_tail_of(g - 1)
        h_tail_of(KD - 1)
        for m in range(KD):
            tails_before(GO0 + min(m + 1 + WD, KD))
            residual("go", m)
        norm(3, A.freed(("go", KD - 1)))

        dve.wait_ge(moe_zero, 1)
        dve.wait_ge(*A.full("rt"))
        v.tensor_copy(lg[:, 0:2, 0:E], A.ap("rt")[:, 0:2 * E].rearrange("p (m e) -> p m e", m=2))
        v.tensor_copy(lg[0:NS, 2, 0:E], A.ap("rt")[0:NS, 2 * E:3 * E]).then_inc(a_dve, 1)
        dve.wait_ge(*A.freed("rt"))
        for m in range(3):
            r = ROWS[m]
            link(v.max(r8[0:r, m, :], lg[0:r, m, 0:E]))
            v.tensor_scalar(cden[0:r, m, 0:1], r8[0:r, m, 0:1], -1.0, None, ALU.mult).then_inc(neg_m1, 1)
            link(v.tensor_copy(l8[0:r, m, 0:2], r8[0:r, m, 0:2]))
            link(v.match_replace(wk[0:r, m, :], l8[0:r, m, :], lg[0:r, m, :], MARK))
            ins = v.tensor_scalar(sel[0:r, m, :], wk[0:r, m, 0:E], MARKED, None, ALU.is_lt)
        ins.then_inc(sel_ok, 1)
        dve.wait_ge(sel_ok, 1)

        def minus(dst, src, head):
            return v.tensor_tensor(dst, src, head.bitcast(F32), ALU.subtract)

        for m in range(3):
            for half in range(2):
                r, part = ROWS[m], slice(CH * half, CH * half + CH)
                dve.wait_ge(hoh_ok, 2 * m + half + 1)
                minus(htokl[0:r, m, part], A.ap(("ho", m, half))[0:r, :], htokh[0:r, m, part]).then_inc(a_dve, 1)
        dve.wait_ge(ex_ok, 3)
        for m in range(3):
            r = ROWS[m]
            link(v.tensor_tensor(ex[0:r, m, :], ex[0:r, m, :], sel[0:r, m, :], ALU.mult))
            link(v.tensor_reduce(cden[0:r, m, 1:2], ex[0:r, m, :], AX.X, ALU.add))
            link(v.reciprocal(cden[0:r, m, 2:3], cden[0:r, m, 1:2]))
            for blk in range(MAXBLK):
                last = v.tensor_scalar(comb[0:r, m, 1 + E * blk:1 + E * blk + E], ex[0:r, m, :], cden[0:r, m, 2:3], None, ALU.mult)
            link(last)
        dve.wait_ge(*A.full("pos"))
        v.tensor_copy(cnt[:, 0:E], A.ap("pos")[:, 3 * E:4 * E])
        v.tensor_copy(pos[:, 0:2, :], A.ap("pos")[:, 0:2 * E].rearrange("p (m e) -> p m e", m=2))
        v.tensor_copy(pos[0:NS, 2, :], A.ap("pos")[0:NS, 2 * E:3 * E]).then_inc(a_dve, 1)
        dve.wait_ge(*A.freed("pos"))
        for m in range(3):
            r = ROWS[m]
            link(v.scalar_tensor_tensor(out=pos[0:r, m, :], in0=pos[0:r, m, :], scalar=FAR, in1=sel[0:r, m, :],
                                        op0=ALU.add, op1=ALU.mult))
            for blk in range(MAXBLK):
                last = v.tensor_scalar(slot_of[0:r, m, E * blk:E * blk + E], pos[0:r, m, :], -FAR - P * blk, None, ALU.add)
            link(last)
        link(v.tensor_reduce(r8[0:1, 0, 0:1], cnt[0:1, 0:E], AX.X, ALU.max))
        link(v.tensor_scalar(r8[0:1, 0, 1:2], r8[0:1, 0, 0:1], float(P), float(E), ALU.is_gt, ALU.mult))
        link(v.tensor_scalar(r8[0:1, 0, 2:3], r8[0:1, 0, 0:1], float(2 * P), float(E), ALU.is_gt, ALU.mult))
        link(v.tensor_tensor(r8[0:1, 0, 3:4], r8[0:1, 0, 1:2], r8[0:1, 0, 2:3], ALU.add))
        v.tensor_scalar(cnt_i[0:1, 0:1], r8[0:1, 0, 3:4], float(E), None, ALU.add).then_inc(items_ok, 1)

        def picks(item):
            for m in range(3):
                r = ROWS[m]
                last = v.tensor_scalar(pick[0:r, m, :], iota[0:r, :], slot_of[0:r, m, bass.ds(item, 1)], None,
                                       ALU.is_equal)
            return last

        picks(0).then_inc(pick_ok, 1)
        dve.wait_ge(items_ok, 1)
        n_items = dve.value_load(cnt_i[0:1, 0:1], min_val=E, max_val=ITEMS)

        def add_back(i, parts=range(6)):
            for k in parts:
                m, half = k // 2, k % 2
                dve.wait_ge(sc_full, i * 6 + (k + 1))
                x = xtok[0:ROWS[m], m, CH * half:CH * half + CH]
                v.scalar_tensor_tensor(out=x, in0=banks[6 + k % 2][0:ROWS[m], :], scalar=comb[0:ROWS[m], m, bass.ds(i, 1)],
                                       in1=x, op0=ALU.mult, op1=ALU.add).then_inc(sc_ok, 1)

        def tails(i, t, quarters=range(QU)):
            for q in quarters:
                k = (QU * t + q) % WRING
                dve.wait_ge(q_head, i * QI + (QU * t + q + 1))
                minus(wq[:, k, 1, :], ring[expert_slot(t)][:, 1024 * q:1024 * q + 1024], wq[:, k, 0, :])\
                    .then_inc(q_tail, 1)

        def gathered_tails(bank, half, n):
            dve.wait_ge(xgh_ok, n)
            part = slice(4 * half, 4 * half + 4)
            minus(xgl[:, part, :], bank[:].rearrange("p (k s) -> p k s", k=4), xgh[:, part, :]).then_inc(xg_ok, 1)

        tails(0, 0)
        for half in range(2):
            gathered_tails(banks[6 + half], half, half + 1)
        with dve.Fori(0, n_items) as i:
            at = i * NCH + NCH

            def hidden(c):
                dve.wait_ge(*after(i, UP, c))
                dve.wait_ge(sg_ok, at + (c + 1))
                v.tensor_tensor(he[:], he[:], banks[2 + c % 2][:], ALU.mult).then_inc(he_ok, 1)

            def heT_tails(c):
                dve.wait_ge(heTh_ok, i * NCH + (c + 1))
                minus(heTl[:], banks[6 + T_BANK[c]][:], heTh[:]).then_inc(heT_ok, 1)

            for t in range(1, PER_ITEM):
                kind, c = TILES[t]
                if t != 2:
                    tails(i, t)
                if t == 1:
                    dve.wait_ge(sc_ok, i * 6 + 6)
                    add_back(i, (0, 1))
                elif t == 2:
                    tails(i, t, (0, 1))
                    add_back(i, (2, 3))
                    tails(i, t, (2, 3))
                    add_back(i, (4, 5))
                if kind == UP and c >= 1:
                    heT_tails(c - 1)
                if t >= 2 and TILES[t - 1][0] == UP:
                    hidden(TILES[t - 1][1])
                if TILES[t] == (GATE, 2):
                    dve.wait_ge(pg_full, i + 2)
                    picks(i + 1).then_inc(pick_ok, 1)
            gathered_tails(banks[7], 0, i * 2 + 3)
            heT_tails(NCH - 1)
            gathered_tails(banks[7], 1, i * 2 + 4)
            tails(i + 1, 0)
            for half in range(2):
                part = slice(CH * half, CH * half + CH)
                dve.wait_ge(yh_ok, i * 2 + (half + 1))
                minus(ysbl[:, part], banks[4 + half][:], ysbh[:, part]).then_inc(y_ok, 1)
        dve.wait_ge(sc_ok, n_items * 6 + 6)
        add_back(n_items)

    @block.tensor
    def _(pe):
        mm = nc.tensor.matmul
        tr = nc.tensor.transpose

        def weights(name):
            pe.wait_ge(*arrived_at[name])

        def ssq(n):
            B.room(pe, ("ssq", n))
            pe.wait_ge(sq_act, n + 1)
            pe.wait_ge(sq_dve, n + 1)
            for c in range(KD):
                last = mm(B.ap(("ssq", n))[:, 0:T], ones[:], hT[:, c, :], start=(c == 0), stop=(c == KD - 1))
            last.then_inc(b_full, 1)

        def project(group, tile, col, ready, rhs=hT, k=KD, width=P, ncols=T):
            A.room(pe, group)
            for c in range(k):
                if ready is not None:
                    pe.wait_ge(ready[0], ready[1] + c)
                last = mm(A.ap(group)[0:width, 0:ncols], tile[:, c, col:col + width], rhs[:, c, 0:ncols],
                          start=(c == 0), stop=(c == k - 1))
            last.then_inc(a_full, 1)


        def three(out, w_h, w_l, x_h, x_l, start, stop, weights_stay=True):
            def product(w, x, **flags):
                return mm(out, w, x, **flags) if weights_stay else mm(out, x, w, **flags)
            product(w_h, x_h, start=start, stop=False)
            read = product(w_h, x_l, start=False, stop=False)
            return read, product(w_l, x_h, start=False, stop=stop)

        def project_split(group, n, tails, ready=None):
            A.room(pe, group)
            pe.wait_ge(*its_tails_ready(n))
            w_h, w_l = its_heads(n), in_tile(n, ring_r)
            for c in range(KD):
                if ready is not None:
                    pe.wait_ge(h_tail, ready + c)
                read, last = three(A.ap(group)[:, 0:T], w_h[:, c, :], w_l[:, c, :], hT_r[:, c, :],
                                   tails[:, c, :], c == 0, c == KD - 1)
            read.then_inc(d_used, 1)
            last.then_inc(a_full, 1)

        def to_tokens(group, src, m, half, ready):
            A.room(pe, group)
            pe.wait_ge(*ready)
            r = ROWS[m]
            for j in range(4):
                last = tr(A.ap(group)[0:r, P * j:P * j + P], src[:, 4 * half + j, P * m:P * m + r], ident[:])
            last.then_inc(a_full, 1)

        def project_tokens_split(name, half, n0, tails, seen=None):
            for m in range(3):
                A.room(pe, (name, m, half))
            for q in range(QU):
                pe.wait_ge(*its_tails_ready(n0 + q))
                if seen is not None:
                    pe.wait_ge(h_tail, seen + 2 * q + 2)
                w_h, w_l = its_heads(n0 + q), in_tile(n0 + q, ring_r)
                for m in range(3):
                    tokens = slice(P * m, P * m + ROWS[m])
                    for j in range(2):
                        c = 2 * q + j
                        read, last = three(A.ap((name, m, half))[0:ROWS[m], :], w_h[:, j, :], w_l[:, j, :],
                                           hT_r[:, c, tokens], tails[:, c, tokens],
                                           c == 0, c == KD - 1, False)
                    if q == QU - 1:
                        last.then_inc(a_full, 1)
                read.then_inc(d_used, 1)

        start_counters(pe, q_used, t_full, pg_full)
        pe.wait_ge(const, 1)
        pe.wait_ge(par_in, 16 * 8)
        tr(A.ap("par")[:, 0:35], small[:], ident[0:35, 0:35]).then_inc(a_full, 1)
        for m in range(3):
            pe.wait_ge(x_in[m], 16)
        for c in range(KD):
            A.room(pe, ("xt", c))
            for m in range(3):
                r = ROWS[m]
                last = tr(A.ap(("xt", c))[:, P * m:P * m + r], tok[0:r, m, P * c:P * c + P], ident[0:r, 0:r])
            last.then_inc(a_full, 1)
        ssq(0)
        weights("qi")
        for p in range(4):
            project(("qi", p), w3("qi"), P * p, (h_ready, 1) if p == 0 else None, hE)
        weights("kiwi")
        kw = w3("kiwi", SMALLW)
        project("ki", kw, 0, None, hE)
        A.room(pe, "wi")
        for m in range(2):
            for c in range(KD):
                mm(A.ap("wi")[:, IH * m:IH * m + IH], hE[:, c, P * m:P * m + P], kw[:, c, 2 * ID:SMALLW],
                   start=(c == 0), stop=(c == KD - 1))
        for c in range(KD):
            last = mm(A.ap("wi")[0:IH, 64:64 + NS], kw[:, c, 2 * ID:SMALLW], hE[:, c, NP:T],
                      start=(c == 0), stop=(c == KD - 1))
        last.then_inc(a_full, 1)
        B.room(pe, "kissq")
        pe.wait_ge(kisq_ok, 1)
        mm(B.ap("kissq")[:, 0:T], ones[:], kisq[:], start=True, stop=True).then_inc(b_full, 1)
        A.room(pe, "wrep")
        pe.wait_ge(*A.freed("wi"))
        pe.wait_ge(const, 2)
        mm(A.ap("wrep")[:, 0:NS], rep8[:], wiT[:], start=True, stop=True).then_inc(a_full, 1)
        pe.wait_ge(kip2_ok, 1)
        for q in range(4):
            A.room(pe, ("kipt", q))
            for j in range(4):
                last = tr(A.ap(("kipt", q))[:, P * j:P * j + P],
                          kip[:, 4 * q + j, :, :].rearrange("p a d -> p (a d)"), ident[:])
            last.then_inc(a_full, 1)
        A.room(pe, "kio")
        pe.wait_ge(*A.freed("ki"))
        for m in range(3):
            last = tr(A.ap("kio")[0:ROWS[m], P * m:P * m + P], kiT[:, P * m:P * m + ROWS[m]], ident[:])
        last.then_inc(a_full, 1)
        pe.wait_ge(*A.freed(("qi", 2)))
        pe.wait_ge(*A.freed(("qi", 3)))
        for g in range(2):
            A.room(pe, ("iss", g))
            for j in range(4):
                b = 4 * g + j
                rows = A.ap(("iss", g))[NS * j:NS * j + NS, :]
                q = qix[:, b, :, :].rearrange("p h t -> p (h t)")
                pe.wait_ge(*A.freed(("kipt", b // 2)))
                mm(rows[:, 0:PAST], q, kipT[:, 2 * b:2 * b + 2, :].rearrange("p a s -> p (a s)"), start=True, stop=True)
                last = mm(rows[:, PAST:WS], q, kiT[:, NP + TS * b:NP + TS * b + TS], start=True, stop=True)
            last.then_inc(a_full, 1)
        A.room(pe, "isel")
        pe.wait_ge(*A.freed("wrep"))
        for g in range(2):
            pe.wait_ge(*A.freed(("iss", g)))
            last = mm(A.ap("isel")[0:NS, 0:WS], selw[:, g, :], rls[:, g, :], start=(g == 0), stop=(g == 1))
        last.then_inc(a_full, 1)
        for g in range(6):
            A.room(pe, ("is", g))
            i = 0 if g < 2 else 1
            w = P * (i + 1)
            per = CH // w
            for j in range(per):
                h = (g if i == 0 else g - 2) * per + j
                last = mm(A.ap(("is", g))[:, w * j:w * j + w], qiz[:, h, P * i:P * i + P], kiT[:, 0:w],
                          start=True, stop=True)
            last.then_inc(a_full, 1)

        def head_ssq(n):
            B.room(pe, ("qkn", n))
            pe.wait_ge(qsq, n + 1)
            mm(B.ap(("qkn", n))[:, 0:T], ones[:], sq2[:, n % 2, :], start=True, stop=True).then_inc(b_full, 1)

        for n in range(16):
            project_split(("qk", n), n, hE_r, 1 if n == 0 else None)
            if n:
                head_ssq(n - 1)
        head_ssq(15)
        for half in range(2):
            project_tokens_split("v", half, VQ0 + QU * half, hE_r)
        for m in range(3):
            for half in range(2):
                to_tokens(("kt", m, half), kT, m, half, A.freed(("qk", 15)))

        def keys_turn(n):
            weights(("kp", n // 4))
            page = ring[slot[("kp", n // 4)]][:, D * (n % 4):D * (n % 4) + D]
            for q in range(2):
                A.room(pe, ("ktr", n, q))
                for j in range(4):
                    h = 4 * q + j
                    last = tr(A.ap(("ktr", n, q))[:, P * j:P * j + P], page[:, P * h:P * h + P], ident[:])
                last.then_inc(a_full, 1)

        def keys_dot(n):
            b, pg = n // 2, n % 2
            pe.wait_ge(*A.freed(("ktr", n, 0)))
            pe.wait_ge(*A.freed(("ktr", n, 1)))
            for h in range(H):
                c0 = H * NS * pg + NS * h + TS * b
                last = mm(B.ap("st")[:, c0:c0 + TS], KT[:, n % 2, h, :], qT[:, h, NP + TS * b:NP + TS * b + TS],
                          start=True, stop=True)
            if n == NPG - 1:
                last.then_inc(b_full, 1)
            else:
                last.then_inc(kt_free, 1)

        B.room(pe, "st")
        B.room(pe, "stn")
        keys_turn(0)
        for b in range(NSEQ):
            if b < NU:
                A.room(pe, ("s", b))
                w = P * (unit_tile[b] + 1)
                for j, h in enumerate(unit_heads[b]):
                    last = mm(A.ap(("s", b))[:, w * j:w * j + w], qT[:, h, P * unit_tile[b]:P * unit_tile[b] + P],
                              kT[:, h, 0:w], start=True, stop=True)
                last.then_inc(a_full, 1)
            keys_turn(2 * b + 1)
            keys_dot(2 * b)
            if 1 <= b <= NU:
                u = b - 1
                A.room(pe, ("pt", u))
                pe.wait_ge(p_ok, u + 1)
                for j in range(4):
                    last = tr(A.ap(("pt", u))[:, P * j:P * j + P], sm[:, u % 2, P * j:P * j + P], ident[:])
                last.then_inc(a_full, 1)
            if 2 * b + 2 < NPG:
                keys_turn(2 * b + 2)
            keys_dot(2 * b + 1)
            if 2 <= b <= NU + 1:
                u = b - 2
                A.room(pe, ("o", u))
                pe.wait_ge(*A.freed(("pt", u)))
                nk = unit_tile[u] + 1
                for j, h in enumerate(unit_heads[u]):
                    for kc in range(nk):
                        last = mm(A.ap(("o", u))[:, P * j:P * j + P], tok[:, kc, P * h:P * h + P],
                                  PT[:, u % 2, P * (nk * j + kc):P * (nk * j + kc) + P],
                                  start=(kc == 0), stop=(kc == nk - 1))
                last.then_inc(a_full, 1)
        for h in range(H):
            last = mm(B.ap("stn")[0:NS, NS * h:NS * h + NS], kT[:, h, NP:T], qT[:, h, NP:T], start=True, stop=True)
        last.then_inc(b_full, 1)
        A.room(pe, "mrep")
        pe.wait_ge(mk_ok, 1)
        mm(A.ap("mrep")[:, 0:PAST + NS], rep32[:], madd_s[:], start=True, stop=True).then_inc(a_full, 1)
        pe.wait_ge(*B.freed("stn"))
        for g in range(2):
            A.room(pe, ("ss", g))
            for pg in range(PAGES):
                tr(A.ap(("ss", g))[:, P * pg:P * pg + P], stS[:, H * NS * pg + P * g:H * NS * pg + P * g + P], ident[:])
            tr(A.ap(("ss", g))[:, PAST:PAST + NS], stN[:, P * g:P * g + P], ident[0:NS, 0:NS]).then_inc(a_full, 1)
        for g in range(2):
            A.room(pe, ("spt", g))
            pe.wait_ge(p_ok, NU + g + 1)
            s = sm[:, (NU + g) % 2, :]
            for pg in range(PAGES):
                tr(A.ap(("spt", g))[:, P * pg:P * pg + P], s[:, P * pg:P * pg + P], ident[:])
            tr(A.ap(("spt", g))[0:NS, PAST:PAST + P], s[:, PAST:PAST + NS], ident[:]).then_inc(a_full, 1)
        B.room(pe, "so")
        so = B.ap("so")
        pe.wait_ge(*A.freed(("spt", 1)))
        for h in range(H):
            g, j = h // 4, h % 4
            mm(so[:, NS * h:NS * h + NS], tok[0:NS, 2, P * h:P * h + P],
               sPT[0:NS, g, 2 * P + NS * j:2 * P + NS * j + NS], start=(h == 0), stop=False, skip_group_check=True)
        for b in range(NSEQ):
            weights(("vp", b // 2))
            for pg in range(PAGES):
                c0 = D * (2 * (b % 2) + pg)
                for h in range(H):
                    g, j = h // 4, h % 4
                    s0 = P * pg + NS * j + TS * b
                    last = mm(so[:, NS * h + TS * b:NS * h + TS * b + TS],
                              ring[slot[("vp", b // 2)]][:, c0 + P * h:c0 + P * h + P], sPT[:, g, s0:s0 + TS],
                              start=False, stop=(b == NSEQ - 1 and pg == PAGES - 1 and h == H - 1),
                              skip_group_check=True)
            if b == NSEQ - 1:
                last.then_inc(b_full, 1)
            elif b % 2:
                last.then_inc(part_used, 1)
        for m in range(KD):
            weights(("wo", m // 4))
            if m == 0:
                pe.wait_ge(*A.freed(("o", NU - 1)))
                pe.wait_ge(*B.freed("so"))
            project(("wo", m), w3(("wo", m // 4)), P * (m % 4), None)

        ssq(1)
        for f in range(NFB):
            project_split(("fg", f), F0 + 2 * f, hL_r, KD + 1 if f == 0 else None)
            project_split(("fu", f), F0 + 2 * f + 1, hL_r)
        n = FD0
        for half in range(2):
            for m in range(4):
                A.room(pe, ("fd", 4 * half + m))
            for part in range(3):
                for q in range(min(8, NFB - 8 * part) // 2):
                    pe.wait_ge(*its_tails_ready(n))
                    w_h, w_l = its_heads(n), in_tile(n, ring_r)
                    for j in range(2):
                        f = 8 * part + 2 * q + j
                        if half == 0:
                            pe.wait_ge(hh_tail, f + 1)
                        for m in range(4):
                            cols_ = slice(P * m, P * m + P)
                            read, last = three(A.ap(("fd", 4 * half + m))[:, 0:T], w_h[:, j, cols_], w_l[:, j, cols_],
                                               hh[:, f, :], hhl_r[:, f, :], f == 0, f == NFB - 1)
                            if f == NFB - 1:
                                last.then_inc(a_full, 1)
                    read.then_inc(d_used, 1)
                    n += 1
                if part < 2:
                    last.then_inc(part_used, 1)

        ssq(2)
        for half in range(2):
            project_tokens_split("gv", half, GV0 + QU * half, hL_r, 2 * KD if half == 0 else None)
        pe.wait_ge(ws_in, 16)
        for q in range(2):
            A.room(pe, ("wst", q))
            for j in range(4):
                last = tr(A.ap(("wst", q))[:, P * j:P * j + P], wsr[:, 4 * q + j, :], ident[:])
            last.then_inc(a_full, 1)
        for c in range(KD):
            project_split(("gu", c), GU0 + c, hL_r)
            if c == 1:
                A.room(pe, "wsr")
                pe.wait_ge(ws_ok, 1)
                mm(A.ap("wsr")[0:NS, 0:8 * TS], rep4[:], wsT[0:TS, :, 0:TS], start=True, stop=True).then_inc(a_full, 1)
        pe.wait_ge(ln_ok, 4)
        pe.wait_ge(wsS_ok, 1)
        for g in range(8):
            A.room(pe, ("mix", g))
            for m in range(3):
                r = ROWS[m]
                mat = wsT[:, g, :] if m < 2 else wsS[:, g, :]
                last = mm(A.ap(("mix", g))[:, P * m:P * m + r], gv[0:r, m, P * g:P * g + P], mat, start=True, stop=True)
            last.then_inc(a_full, 1)
        for m in range(KD):
            project_split(("go", m), GO0 + m, hL_r, 3 * KD + 1 if m == 0 else None)

        ssq(3)
        for m in range(3):
            for half in range(2):
                to_tokens(("xo", m, half), xT, m, half, A.freed(("go", KD - 1)))
        A.room(pe, "rt")
        pe.wait_ge(h_ready, 4 * KD)
        pe.wait_ge(wr_in, 16)
        for m in range(3):
            r = ROWS[m]
            for c in range(KD):
                last = mm(A.ap("rt")[0:r, E * m:E * m + E], hT[:, c, P * m:P * m + r], wr[:, c, :],
                          start=(c == 0), stop=(c == KD - 1))
        last.then_inc(a_full, 1)
        for m in range(3):
            for half in range(2):
                to_tokens(("ho", m, half), hT, m, half, (h_ready, 4 * KD))
        A.room(pe, "pos")
        pe.wait_ge(sel_ok, 1)
        for m in range(4):
            r = ROWS[m] if m < 3 else P
            parts = list(range(min(m, 2) + 1)) if m < 3 else [0, 1, 2]
            for k in parts:
                kr = ROWS[k]
                left = upper[0:kr, 0:r] if k == m else ones[0:kr, 0:r]
                last = mm(A.ap("pos")[0:r, E * m:E * m + E], left, sel[0:kr, k, :], start=(k == 0), stop=(k == parts[-1]))
        last.then_inc(a_full, 1)

        def gather(half, bank):
            for j in range(4):
                c = 4 * half + j
                for m in range(3):
                    r = ROWS[m]
                    mm(bank[:, P * j:P * j + P], htokh[0:r, m, P * c:P * c + P], pick[0:r, m, :],
                       start=(m == 0), stop=False)
                    last = mm(bank[:, P * j:P * j + P], htokl[0:r, m, P * c:P * c + P], pick[0:r, m, :],
                              start=False, stop=(m == 2))
            last.then_inc(ga_full, 1)

        def scatter(waits, parts=range(6)):
            for k in parts:
                m, half = k // 2, k % 2
                pe.wait_ge(*waits[k])
                part, left = slice(CH * half, CH * half + CH), pickT[:, P * m:P * m + P]
                mm(banks[6 + k % 2][:], left, ysbh[:, part], start=True, stop=False)
                mm(banks[6 + k % 2][:], left, ysbl[:, part], start=False, stop=True).then_inc(sc_full, 1)

        pe.wait_ge(*A.freed(("ho", 2, 1)))
        pe.wait_ge(pick_ok, 1)
        pe.wait_ge(*B.freed(("ssq", 3)))
        gather(0, banks[6])
        gather(1, banks[7])
        pe.wait_ge(moe_zero, 1)
        pe.wait_ge(*A.freed("pos"))
        pe.wait_ge(items_ok, 1)
        n_items = pe.value_load(cnt_i[0:1, 0:1], min_val=E, max_val=ITEMS)
        with pe.Fori(0, n_items) as i:
            at = i * NCH + NCH
            def three(outs, t, q, stay_h, stay_l, start, stop):
                pe.wait_ge(q_tail, i * QI + (QI + QU * t + q + 1))
                k = (QU * t + q) % WRING
                for n, bank in enumerate(outs):
                    cols_ = slice(CH * n, CH * n + CH)
                    h, l = (stay_h, stay_l) if len(stay_h) == 1 else ([stay_h[n]], [stay_l[n]])
                    first, final = start if isinstance(start, bool) else start[n], stop if isinstance(stop, bool) else stop[n]
                    mm(bank, h[0], wq[:, k, 0, cols_], start=first, stop=False)
                    mm(bank, h[0], wq[:, k, 1, cols_], start=False, stop=False)
                    last = mm(bank, l[0], wq[:, k, 0, cols_], start=False, stop=final)
                last.then_inc(q_used, 1)

            def gate_up(c, kind, between={}):
                free = (sg_ok, he_ok)[kind]
                if c == 0:
                    pe.wait_ge(free, at)
                elif c >= 2:
                    pe.wait_ge(free, at + (c - 1))
                t, bank = TILES.index((kind, c)), banks[2 * kind + c % 2][:]
                for q in range(QU):
                    three([bank, bank], t, q, [xgh[:, 2 * q, :], xgh[:, 2 * q + 1, :]],
                          [xgl[:, 2 * q, :], xgl[:, 2 * q + 1, :]], [q == 0, False], [False, q == QU - 1])
                    if q in between:
                        scatter(back, between[q])

            def turn(c, free):
                pe.wait_ge(he_ok, at + (c + 1))
                pe.wait_ge(*free)
                bank = banks[6 + T_BANK[c]]
                for j in range(4):
                    last = tr(bank[:, P * j:P * j + P], he[:, P * j:P * j + P], ident[:])
                last.then_inc(t_full, 1)

            def down(c):
                pe.wait_ge(heT_ok, at + (c + 1))
                if c == 0:
                    pe.wait_ge(y_ok, i * 2 + 2)
                for q in range(QU):
                    part = slice(P * q, P * q + P)
                    three([banks[4][:], banks[5][:]], TILES.index((DOWN, c)), q, [heTh[:, part]], [heTl[:, part]], c == 0 and q == 0, c == NCH - 1 and q == QU - 1)

            pe.wait_ge(xg_ok, i * 2 + 2)
            gate_up(0, 0)
            pe.wait_ge(y_ok, i * 2 + 2)
            pe.wait_ge(pickT_ok, i + 1)
            back = [(heT_ok, at), (xg_ok, i * 2 + 2)] + [(sc_ok, i * 6 + (k + 5)) for k in range(2, 6)]
            scatter(back, (0, 1))
            gate_up(0, 1, {1: (2, 3), 3: (4, 5)})
            for c in range(1, NCH):
                gate_up(c, 0)
                free = {0: (sc_ok, i * 6 + 11), 1: (heT_ok, at + 1), 2: (pickT_ok, i + 2)}
                turn(c - 1, free.get(c - 1, (heT_ok, at + (c - 2))))
                if c == 1:
                    pe.wait_ge(sc_ok, i * 6 + 12)
                    for m in range(3):
                        r = ROWS[m]
                        last = tr(banks[7][:, P * m:P * m + r], pick[0:r, m, :].bitcast(F32), ident[0:r, 0:r])
                    last.then_inc(pg_full, 1)
                gate_up(c, 1)
                down(c - 1)
            pe.wait_ge(pick_ok, i + 2)
            pe.wait_ge(heT_ok, at + 5)
            gather(0, banks[7])
            turn(NCH - 1, (heT_ok, at + 6))
            pe.wait_ge(xg_ok, i * 2 + 3)
            gather(1, banks[7])
            down(NCH - 1)
        pe.wait_ge(y_ok, n_items * 2 + 2)
        pe.wait_ge(pickT_ok, n_items + 1)
        scatter([(heT_ok, n_items * NCH + NCH), (xg_ok, n_items * 2 + 2)]
                + [(sc_ok, n_items * 6 + (k + 5)) for k in range(2, 6)])

    return ctx


T_BANK = [0, 0, 1, 0, 1, 0, 0]


INS = ["x_prompt", "x_sample", "cache_k", "cache_v", "cache_kidx", "page_table", "norm_mix", "norm_ffn",
       "attn_w_in", "attn_g_q", "attn_g_k", "attn_g_kidx", "attn_w_out", "gm_w_in", "gm_ln_g", "gm_ln_b",
       "gm_w_s", "gm_b_s", "gm_w_out", "ffn_w_gate", "ffn_w_up", "ffn_w_down", "moe_w_router", "moe_w_gate",
       "moe_w_up", "moe_w_down"]
OUTS = {
    "y_prompt": (1, NP, D), "y_sample": (NSEQ, TS, D),
    "k_prompt": (1, NP // P, P, H, HD), "v_prompt": (1, NP // P, P, H, HD), "kidx_prompt": (1, NP // P, P, ID),
    "k_sample": (1, NSEQ, TS, H, HD), "v_sample": (1, NSEQ, TS, H, HD), "kidx_sample": (1, NSEQ, TS, ID),
    "gm_v_sample": (1, NSEQ, TS, D),
}


def kernel(**inputs):
    import numpy as np
    import concourse.bacc as bacc
    from concourse.bass_utils import run_bass_kernel_spmd

    nc = bacc.Bacc("TRN2", target_bir_lowering=False, num_devices=1)
    arrays, ins, outs = {}, {}, {}
    for name in INS:
        x = np.ascontiguousarray(inputs[name])
        arrays[f"in_{name}"] = x
        ins[name] = nc.dram_tensor(f"in_{name}", x.shape, mybir.dt.from_np(x.dtype), kind="ExternalInput").ap()
    for name, shape in OUTS.items():
        outs[name] = nc.dram_tensor(f"out_{name}", shape, F32, kind="ExternalOutput").ap()
    with build(nc, ins, outs):
        pass
    r = run_bass_kernel_spmd(nc, [arrays], core_ids=[0])
    return tuple(r.results[0][f"out_{name}"] for name in OUTS)
```
